# Optimizing a Trainium2 kernel written in Bass

```python
import math
import jax, jax.numpy as jnp
from jax import lax
import numpy as np

D_MODEL = 1024
BATCH = 1
SEQ = 512
DEPTH = 1
DEC_BATCH = 1
DEC_SEQ = 32
PAST_LEN = 128

CHUNK = 64
SSM_WIDTH = D_MODEL // 2
SSM_GROUP = 16
SSM_GROUPS = SSM_WIDTH // SSM_GROUP
SSM_STATE = 64
DT_MIN = 1e-3
DT_MAX = 1e-1
POOL_WIDTH = D_MODEL // 2
POOL_WINDOWS = (2, 4, 8, 16)
POOL_GROUPS = len(POOL_WINDOWS)
POOL_GROUP_IN = POOL_WIDTH // POOL_GROUPS
POOL_GROUP_OUT = D_MODEL // POOL_GROUPS
POOL_HIST = max(POOL_WINDOWS) - 1
N_BRANCHES = 2
IN_WIDTH = SSM_WIDTH + POOL_WIDTH + N_BRANCHES * D_MODEL
N_EXPERT_GROUPS = 4
EXPERTS_PER_GROUP = 8
N_EXPERTS = N_EXPERT_GROUPS * EXPERTS_PER_GROUP
TOP_K_INNER = 2
D_EXPERT = D_MODEL // 2
EPS = 1e-6

kernel_name = 'hybrid_s5_pool_hmoe_stream_step'

def _rmsnorm(x, g):
    xf = x.astype(jnp.float32)
    r = lax.rsqrt(jnp.mean(xf * xf, axis=-1, keepdims=True) + EPS)
    return (xf * r * g.astype(jnp.float32)).astype(x.dtype)

def _ssm_discretise(a_re, a_im, log_dt, b_re, b_im):
    lam_re = jnp.minimum(a_re.astype(jnp.float32), -1e-4)
    lam_im = a_im.astype(jnp.float32)
    dt = jnp.exp(log_dt.astype(jnp.float32))[:, None]
    mag = jnp.exp(lam_re * dt)
    ang = lam_im * dt
    abar_re = mag * jnp.cos(ang)
    abar_im = mag * jnp.sin(ang)
    num_re = abar_re - 1.0
    num_im = abar_im
    den = lam_re * lam_re + lam_im * lam_im
    k_re = (num_re * lam_re + num_im * lam_im) / den
    k_im = (num_im * lam_re - num_re * lam_im) / den
    br = b_re.astype(jnp.float32)
    bi = b_im.astype(jnp.float32)
    bbar_re = k_re[..., None] * br - k_im[..., None] * bi
    bbar_im = k_re[..., None] * bi + k_im[..., None] * br
    return abar_re, abar_im, bbar_re, bbar_im

def _scan_combine(e1, e2):
    a1r, a1i, b1r, b1i = e1
    a2r, a2i, b2r, b2i = e2
    ar = a2r * a1r - a2i * a1i
    ai = a2r * a1i + a2i * a1r
    br = a2r * b1r - a2i * b1i + b2r
    bi = a2r * b1i + a2i * b1r + b2i
    return ar, ai, br, bi

def _ssm_branch(u, h0_re, h0_im, abar_re, abar_im, bbar_re, bbar_im, c_re, c_im, d, w_glu_a, w_glu_b):
    b, l, _ = u.shape
    uf = u.astype(jnp.float32).reshape(b, l, SSM_GROUPS, SSM_GROUP)
    bu_re = jnp.einsum('blgp,gnp->blgn', uf, bbar_re)
    bu_im = jnp.einsum('blgp,gnp->blgn', uf, bbar_im)
    h0r = h0_re.astype(jnp.float32)
    h0i = h0_im.astype(jnp.float32)
    bu_re = bu_re.at[:, 0].add(abar_re * h0r - abar_im * h0i)
    bu_im = bu_im.at[:, 0].add(abar_re * h0i + abar_im * h0r)
    a_re = jnp.broadcast_to(abar_re, bu_re.shape)
    a_im = jnp.broadcast_to(abar_im, bu_im.shape)
    _, _, h_re, h_im = lax.associative_scan(_scan_combine, (a_re, a_im, bu_re, bu_im), axis=1)
    y = (jnp.einsum('blgn,gpn->blgp', h_re, c_re.astype(jnp.float32))
         - jnp.einsum('blgn,gpn->blgp', h_im, c_im.astype(jnp.float32))
         + d.astype(jnp.float32) * uf)
    g = jax.nn.gelu(y.reshape(b, l, SSM_WIDTH)).astype(u.dtype)
    out = (g @ w_glu_a) * jax.nn.sigmoid(g @ w_glu_b)
    return out, h_re[:, -1], h_im[:, -1]

def _pool_branch(u, hist, start, pool_w, pool_scale):
    b, l, _ = u.shape
    uf = u.astype(jnp.float32)
    xp = jnp.concatenate([hist.astype(jnp.float32), uf], axis=1)
    cs = jnp.cumsum(xp, axis=1)
    cs0 = jnp.concatenate([jnp.zeros((b, 1, POOL_WIDTH), jnp.float32), cs], axis=1)
    pos = start + jnp.arange(l)
    pooled = []
    for gi, w in enumerate(POOL_WINDOWS):
        c0, c1 = gi * POOL_GROUP_IN, (gi + 1) * POOL_GROUP_IN
        hi = cs0[:, POOL_HIST + 1:, c0:c1]
        lo = cs0[:, POOL_HIST + 1 - w:POOL_HIST + 1 - w + l, c0:c1]
        cnt = jnp.minimum(w, pos + 1).astype(jnp.float32)[None, :, None]
        pooled.append((hi - lo) / cnt)
    pooled = jnp.stack(pooled, axis=2)
    z = (pooled - uf.reshape(b, l, POOL_GROUPS, POOL_GROUP_IN)).astype(u.dtype)
    o = jnp.einsum('blgc,gcd->blgd', z, pool_w).reshape(b, l, D_MODEL) * pool_scale
    return o, xp[:, -POOL_HIST:].astype(u.dtype)

def _hmoe(x, g, w_router_group, w_router_expert, w_gate, w_up, w_down):
    b, l, dm = x.shape
    xn = _rmsnorm(x, g).reshape(b * l, dm)
    n = b * l
    lg = (xn @ w_router_group).astype(jnp.float32)
    pg = jax.nn.softmax(lg, axis=-1)
    grp = jnp.argmax(lg, axis=-1)
    wg = jnp.max(pg, axis=-1)
    le = jnp.einsum('nd,dge->nge', xn, w_router_expert).astype(jnp.float32)
    le_sel = le[jnp.arange(n), grp]
    top_v, top_i = lax.top_k(le_sel, TOP_K_INNER)
    wk = jax.nn.softmax(top_v, axis=-1) * wg[:, None]
    eidx = grp[:, None] * EXPERTS_PER_GROUP + top_i
    combine = jnp.sum(jax.nn.one_hot(eidx, N_EXPERTS, dtype=jnp.float32) * wk[..., None], axis=1)
    y = jnp.zeros((n, dm), jnp.float32)
    for e in range(N_EXPERTS):
        h = jax.nn.silu(xn @ w_gate[e]) * (xn @ w_up[e])
        y = y + combine[:, e:e + 1] * (h @ w_down[e]).astype(jnp.float32)
    return x + y.reshape(b, l, dm).astype(x.dtype)

def setup_inputs(seed: int = 0) -> dict:
    key = jax.random.key(seed)
    ks = jax.random.split(key, 26)
    f32 = jnp.float32
    nrm = lambda k, s, sc: jax.random.normal(k, s, f32) * sc
    n_idx = jnp.arange(SSM_STATE, dtype=f32)
    return {
        'x_prompt': nrm(ks[0], (BATCH, SEQ, D_MODEL), 1.0),
        'x_sample': nrm(ks[1], (DEC_BATCH, DEC_SEQ, D_MODEL), 1.0),
        'state_ssm_re': nrm(ks[2], (DEPTH, DEC_BATCH, SSM_GROUPS, SSM_STATE), 0.1),
        'state_ssm_im': nrm(ks[3], (DEPTH, DEC_BATCH, SSM_GROUPS, SSM_STATE), 0.1),
        'cache_pool': nrm(ks[4], (DEPTH, DEC_BATCH, POOL_HIST, POOL_WIDTH), 1.0),
        'g_mix': 1.0 + nrm(ks[5], (DEPTH, D_MODEL), 0.02),
        'w_in': nrm(ks[6], (DEPTH, D_MODEL, IN_WIDTH), D_MODEL ** -0.5),
        'ssm_a_re': -0.5 + nrm(ks[7], (DEPTH, SSM_GROUPS, SSM_STATE), 0.01),
        'ssm_a_im': math.pi * n_idx + nrm(ks[8], (DEPTH, SSM_GROUPS, SSM_STATE), 0.01),
        'ssm_log_dt': jax.random.uniform(ks[9], (DEPTH, SSM_GROUPS), f32, math.log(DT_MIN), math.log(DT_MAX)),
        'ssm_b_re': nrm(ks[10], (DEPTH, SSM_GROUPS, SSM_STATE, SSM_GROUP), (2 * SSM_GROUP) ** -0.5),
        'ssm_b_im': nrm(ks[11], (DEPTH, SSM_GROUPS, SSM_STATE, SSM_GROUP), (2 * SSM_GROUP) ** -0.5),
        'ssm_c_re': nrm(ks[12], (DEPTH, SSM_GROUPS, SSM_GROUP, SSM_STATE), SSM_STATE ** -0.5),
        'ssm_c_im': nrm(ks[13], (DEPTH, SSM_GROUPS, SSM_GROUP, SSM_STATE), SSM_STATE ** -0.5),
        'ssm_d': nrm(ks[14], (DEPTH, SSM_GROUPS, SSM_GROUP), 1.0),
        'w_glu_a': nrm(ks[15], (DEPTH, SSM_WIDTH, D_MODEL), SSM_WIDTH ** -0.5),
        'w_glu_b': nrm(ks[16], (DEPTH, SSM_WIDTH, D_MODEL), SSM_WIDTH ** -0.5),
        'pool_w': nrm(ks[17], (DEPTH, POOL_GROUPS, POOL_GROUP_IN, POOL_GROUP_OUT), POOL_GROUP_IN ** -0.5),
        'pool_scale': 1.0 + nrm(ks[18], (DEPTH, D_MODEL), 0.02),
        'w_out': nrm(ks[19], (DEPTH, D_MODEL, D_MODEL), D_MODEL ** -0.5),
        'g_ffn': 1.0 + nrm(ks[20], (DEPTH, D_MODEL), 0.02),
        'w_router_group': nrm(ks[21], (DEPTH, D_MODEL, N_EXPERT_GROUPS), D_MODEL ** -0.5),
        'w_router_expert': nrm(ks[22], (DEPTH, D_MODEL, N_EXPERT_GROUPS, EXPERTS_PER_GROUP), D_MODEL ** -0.5),
        'w_exp_gate': nrm(ks[23], (DEPTH, N_EXPERTS, D_MODEL, D_EXPERT), D_MODEL ** -0.5),
        'w_exp_up': nrm(ks[24], (DEPTH, N_EXPERTS, D_MODEL, D_EXPERT), D_MODEL ** -0.5),
        'w_exp_down': nrm(ks[25], (DEPTH, N_EXPERTS, D_EXPERT, D_MODEL), D_EXPERT ** -0.5),
        'g_final': 1.0 + nrm(jax.random.fold_in(key, 99), (D_MODEL,), 0.02),
    }

def reference(x_prompt, x_sample, state_ssm_re, state_ssm_im, cache_pool, g_mix, w_in, ssm_a_re, ssm_a_im,
              ssm_log_dt, ssm_b_re, ssm_b_im, ssm_c_re, ssm_c_im, ssm_d, w_glu_a, w_glu_b, pool_w, pool_scale,
              w_out, g_ffn, w_router_group, w_router_expert, w_exp_gate, w_exp_up, w_exp_down, g_final):
    assert x_sample.shape[1] <= CHUNK
    disc = [_ssm_discretise(ssm_a_re[li], ssm_a_im[li], ssm_log_dt[li], ssm_b_re[li], ssm_b_im[li])
            for li in range(DEPTH)]

    def trunk(x, h_re, h_im, hist, start):
        new_re, new_im, new_hist = [], [], []
        for li in range(DEPTH):
            abar_re, abar_im, bbar_re, bbar_im = disc[li]
            xn = _rmsnorm(x, g_mix[li])
            proj = xn @ w_in[li]
            u_s = proj[..., :SSM_WIDTH]
            u_p = proj[..., SSM_WIDTH:SSM_WIDTH + POOL_WIDTH]
            gate_s = proj[..., SSM_WIDTH + POOL_WIDTH:SSM_WIDTH + POOL_WIDTH + D_MODEL]
            gate_p = proj[..., SSM_WIDTH + POOL_WIDTH + D_MODEL:]
            o_s, hr, hi = _ssm_branch(u_s, h_re[li], h_im[li], abar_re, abar_im, bbar_re, bbar_im,
                                      ssm_c_re[li], ssm_c_im[li], ssm_d[li], w_glu_a[li], w_glu_b[li])
            o_p, nh = _pool_branch(u_p, hist[li], start, pool_w[li], pool_scale[li])
            merged = jax.nn.sigmoid(gate_s) * o_s + jax.nn.sigmoid(gate_p) * o_p
            x = x + merged @ w_out[li]
            x = _hmoe(x, g_ffn[li], w_router_group[li], w_router_expert[li],
                      w_exp_gate[li], w_exp_up[li], w_exp_down[li])
            new_re.append(hr)
            new_im.append(hi)
            new_hist.append(nh)
        return _rmsnorm(x, g_final), jnp.stack(new_re), jnp.stack(new_im), jnp.stack(new_hist)

    bp = x_prompt.shape[0]
    zero_state = jnp.zeros((DEPTH, bp, SSM_GROUPS, SSM_STATE), jnp.float32)
    zero_hist = jnp.zeros((DEPTH, bp, POOL_HIST, POOL_WIDTH), x_prompt.dtype)
    y_prompt, re_p, im_p, hist_p = trunk(x_prompt, zero_state, zero_state, zero_hist, 0)
    y_sample, re_s, im_s, hist_s = trunk(x_sample, state_ssm_re, state_ssm_im, cache_pool, PAST_LEN)
    sd = state_ssm_re.dtype
    cd = cache_pool.dtype
    return (y_prompt, y_sample, re_p.astype(sd), im_p.astype(sd), hist_p.astype(cd),
            re_s.astype(sd), im_s.astype(sd), hist_s.astype(cd))


_drawn_inputs = setup_inputs


def setup_inputs(seed=0):
    import zlib

    import numpy as np

    out = dict(_drawn_inputs(seed))
    spreads = {}
    factors = {'ssm_a_re': 4.435,
     'ssm_c_re': 2.732,
     'pool_scale': 3.183,
     'g_ffn': 3.255,
     'g_final': 2.848}
    for name, (base, spread) in spreads.items():
        noise = np.random.default_rng([zlib.crc32(name.encode()), seed]).standard_normal(out[name].shape)
        drawn = base * np.exp(spread * noise) if base else spread * noise
        out[name] = __import__('jax').numpy.asarray(drawn.astype(out[name].dtype))
    for name, factor in factors.items():
        out[name] = (out[name] * factor).astype(out[name].dtype)
    return out
```

```python
from contextlib import ExitStack

import concourse.bass as bass
from concourse import mybir

ALU = mybir.AluOpType
ACT = mybir.ActivationFunctionType
F32 = mybir.dt.float32
I32 = mybir.dt.int32
X = mybir.AxisListType.X

P = 128
D = 1024
SEQ, DEC = 512, 32
NT = SEQ + DEC
TT = 5
ROWS = [128, 128, 128, 128, 32]
KD = D // P
L = 8
NC = NT // L
PC = SEQ // L
G, N, Q = 32, 64, 16
NJ = G // 2
HIST = 15
WINDOWS = (2, 4, 8, 16)
NE, EG, EI = 32, 4, 8
F = 512
TILE = 64
EXTRA = (NT + TILE - 1) // TILE - 1
EPS = 1e-6
BIG = 3.0e38
MAIN = NE * TILE
NROWS = -(-(MAIN + 2 * NT + TILE) // P) * P
ZEROED = NROWS // P + (NROWS - MAIN) // P
HALF = NT // 2

SLOT = 4096
RING = 6 * SLOT
O_TOEP, O_ST, O_SNAT, O_UC = 2 * SLOT, 3 * SLOT, 4 * SLOT, 5 * SLOT
O_GC = O_SNAT
O_HPAD = O_UC
O_SGP = O_TOEP
O_GT = O_SGP + 8 * NT
O_POOLW = O_GT + 4 * NT
O_XTOK = RING + 256
O_GB = O_XTOK + TT * D
O_MISC = O_GB + D
O_XNT = O_MISC + 1728
O_MT = O_XNT
O_SGS = O_XNT + KD * NT
O_CPOW = O_SGS + KD * NT
O_UPT = O_CPOW
UPW = HIST + SEQ + HIST + DEC
O_Z = O_UPT + 4 * UPW
O_UT = O_CPOW + 2 * NJ * 9 * Q
O_USQ = O_UT + 4 * NT
O_V = O_USQ + G * NC
O_WR = O_V + NJ * 2 * NC
END = O_WR + 8 * 36
O_XN2 = O_SGS
O_XN2T = O_XN2 + TT * D
O_JUNK = O_XN2T + KD * NT
O_ROUT = O_JUNK + D
M_ID, M_PAR, M_HIST, M_PW, M_A4, M_TMP, M_SS, M_FIN, M_TRI, M_INV, M_MASK, M_EB = (
    0, 128, 228, 288, 576, 640, 1120, 1152, 1280, 1408, 1472, 1504)
M_ONES = 1600

TASKS = [("par", "dve")] + [(f"xt{i}", "act") for i in range(TT)]
TASKS += [(f"u{m}", "act") for m in range(4)] + [(f"gs{m}", "act") for m in range(4)]
TASKS += [("kt", "dve")] + [(f"st{r}", "act") for r in range(4)]
TASKS += [(f"uc{r}", "dve") for r in range(4)] + [(f"usq{r}", "act") for r in range(4)]
TASKS += [(f"v{r}", "dve") for r in range(3)] + [(f"gs{m}", "act") for m in range(4, 8)]
TASKS += [(f"y{r}", "act") for r in range(4)] + [(f"gt{b}", "dve") for b in range(4)]
TASKS += [("fin", "dve")] + [(f"up{m}", "act") for m in range(4)] + [("hist", "act")]
TASKS += [(f"gp{m}", "act") for m in range(8)]
for _m in range(8):
    TASKS += [(f"gb{_m}", "act"), (f"ga{_m}", "dve"), (f"po{_m}", "dve")]
TASKS += [("out0", "dve"), ("out1", "dve"), ("x2t0", "act"), ("out2", "dve"), ("x2t1", "act"),
          ("out3", "dve"), ("x2t2", "act"), ("out4", "dve"), ("x2t3", "act"), ("x2t4", "act"),
          ("lg", "dve"), ("rank", "dve")]
NUM = {name: i for i, (name, _) in enumerate(TASKS)}


def emptied_by(owner, i):
    return sum(1 for _, o in TASKS[:i + 1] if o == owner)


def encoder_step(nc, a, out):
    ctx = ExitStack()
    with ctx:
        arena = ctx.enter_context(nc.sbuf_tensor("arena", [P, END], F32))
        ps = ctx.enter_context(nc.psum_tensor("ps", [P, 8, 512], F32))
        x_rows = nc.dram_tensor("x_rows", (NROWS, D), F32).ap()
        y_rows = nc.dram_tensor("y_rows", (NROWS, D), F32).ap()
        kd = nc.dram_tensor("k_taps", (P, 512), F32).ap()

        def sem(name):
            return ctx.enter_context(nc.semaphore(name))

        def at(offset, words, rows=P, row0=0):
            return arena[row0:row0 + rows, offset:offset + words]

        def misc(offset, words, rows=P, row0=0):
            return at(O_MISC + offset, words, rows, row0)

        def slot(s):
            return at(s * SLOT, SLOT)

        def pair(i):
            return ps[:, 2 * (i % 4):2 * (i % 4) + 2, :]

        ident, tri = misc(M_ID, 128), misc(M_TRI, 128)
        prm = misc(M_PAR, 92)
        hist_t = misc(M_HIST, 60).rearrange("p (g c) -> p g c", g=4)
        powers = misc(M_PW, 288).rearrange("p (r t j) -> p r t j", r=2, t=9)
        a4 = misc(M_A4, 64).rearrange("p (j o i) -> p j o i", j=NJ, o=2)
        ss, rstd = misc(M_SS, TT), misc(M_SS + 8, TT)
        fin_cols = misc(M_FIN, 64)
        inv = misc(M_INV, 60).rearrange("p (g c) -> p g c", g=4)
        diag16 = misc(M_MASK, 16)
        ebase = misc(M_EB, 32)
        ones = misc(M_ONES, P)
        x_tok = at(O_XTOK, TT * D).rearrange("p (i d) -> p i d", i=TT)
        g_b = at(O_GB, D)
        xn_t = at(O_XNT, KD * NT).rearrange("p (k t) -> p k t", k=KD)
        sgs = at(O_SGS, 8 * NT).rearrange("p (m t) -> p m t", m=8)
        sgp = at(O_SGP, 8 * NT).rearrange("p (m t) -> p m t", m=8)
        m_t = at(O_MT, 8 * NT).rearrange("p (m t) -> p m t", m=8)
        u_t = at(O_UT, 4 * NT).rearrange("p (m t) -> p m t", m=4)
        up_t = at(O_UPT, 4 * UPW).rearrange("p (g c) -> p g c", g=4)
        z_t = at(O_Z, 4 * NT).rearrange("p (g t) -> p g t", g=4)
        cpow = [at(O_CPOW + r * NJ * 144, NJ * 144) for r in range(2)]
        usq, v_all = at(O_USQ, G * NC), at(O_V, NJ * 2 * NC)
        v = v_all.rearrange("p (j r c) -> p j r c", j=NJ, r=2)
        s_nat, s_t = at(O_SNAT, 32 * P), at(O_ST, 32 * P)
        toep = at(O_TOEP, G * P)
        uc = at(O_UC, L * 512)
        gc = at(O_GC, L * 512)
        hpad = at(O_HPAD, NJ * 4 * NC).rearrange("p (j r g c) -> p j r g c", j=NJ, r=2, g=2)
        g_t = at(O_GT, 4 * NT).rearrange("p (b t) -> p b t", b=4)
        pool_w = at(O_POOLW, D)
        par_rows = at(O_UT, 128, 92)
        dt_rows = at(O_UT + 128, 2, NJ, 64)
        c_in = at(O_USQ, 512)
        c_t = at(O_USQ + 512, 512).rearrange("p (r j q) -> p r j q", r=2, j=NJ)
        bbd = at(O_USQ + 1024, 1024)
        b_in = at(O_V, 512).rearrange("p (r j q) -> p r j q", r=2, j=NJ)
        bbar = at(O_V + 512, 512).rearrange("p (r j q) -> p r j q", r=2, j=NJ)
        k_sb = at(O_V + 1024, 512)
        cache_rows = at(O_UT + 256, 512, HIST)
        prod = at(O_ST, NJ * 144)
        zeros = at(O_UC, D)
        xn_row = [at(O_UC + D, D), at(O_UC + 2 * D, D)]
        junk0 = at(O_UC + 3 * D, D)
        scan_tmp = at(O_UT, 64).rearrange("p (j o i) -> p j o i", j=NJ, o=2)
        scan_red = at(O_UT + 64, 32).rearrange("p (j o) -> p j o", j=NJ)
        sig_b = [at(O_UT + n * NT, NT) for n in range(2)]
        t1 = [at(O_UT + (2 + n) * NT, NT) for n in range(2)]
        t2 = [at(O_UT + (4 + n) * NT, NT) for n in range(2)]
        win = [at(O_UT + 6 * NT + n * UPW, UPW) for n in range(2)]
        fin_rows = at(O_UT + 8 * NT + 64, 128, 64)
        hist_rows = at(O_UT + 8 * NT + 256, 2 * 512, HIST)
        w_r = at(O_WR, 8 * 36).rearrange("p (k n) -> p k n", k=KD)
        xn2 = at(O_XN2, TT * D).rearrange("p (i d) -> p i d", i=TT)
        xn2_t = at(O_XN2T, KD * NT).rearrange("p (k t) -> p k t", k=KD)
        junk1 = at(O_JUNK, D)
        xg = [at(O_MT + n * D, D, TILE) for n in range(2)]
        xg_t = [at(O_MT + (2 + n) * D, KD * TILE) for n in range(2)]
        silu = [at(O_XN2T + n * F, F, TILE) for n in range(2)]
        h = [at(O_XN2T + (2 + n) * F, F, TILE) for n in range(2)]
        h_t = [at(O_XN2T + (4 + n) * F, 4 * TILE) for n in range(2)]
        y_sb = [at(O_XN2T + 6 * F + n * D, D, TILE) for n in range(2)]
        assert 6 * F + 2 * D <= KD * NT + D
        GATE, UP, DOWN = (4, 3), (5, 0), (2, 1)

        place = [O_ROUT]

        def small(*shape):
            words = 1
            for s in shape:
                words *= s
            ap = at(place[0], words)
            place[0] += words
            assert place[0] <= O_WR
            if len(shape) == 2:
                return ap.rearrange("p (a b) -> p a b", a=shape[0])
            if len(shape) == 3:
                return ap.rearrange("p (a b c) -> p a b c", a=shape[0], b=shape[1])
            if len(shape) == 4:
                return ap.rearrange("p (a b c d) -> p a b c d", a=shape[0], b=shape[1], c=shape[2])
            return ap

        logits = small(TT, 36)
        onehot = [small(TT, NE) for _ in range(2)]
        chosen = small(TT, NE)
        weight = small(TT, 2)
        rows_f = small(TT, 2)
        rows_i = small(TT, 2).bitcast(I32)
        ranks = small(TT, NE)
        s_a, s_b, s_c, s_d = (small(TT) for _ in range(4))
        g_hot, g_exp = small(TT, EG), small(TT, EG)
        le_sel, i_hot = small(TT, EI), [small(TT, EI) for _ in range(2)]
        i_tmp = small(TT, EI)
        le_mul = small(TT, EG, EI)
        prefer = small(EI)
        counts = small(NE)
        tab_f = small(2, EXTRA, NE)
        rank_mul = small(TT, NE)
        e_neg = small(TT)
        table = small(2 * NE * EXTRA + 8)[0:1].bitcast(I32)

        x_in, small_in, b_loaded, c_loaded = sem("x_in"), sem("small_in"), sem("b_loaded"), sem("c_loaded")
        dt_ready = sem("dt_ready")
        g_in, w_stream, pw_in, wr_in = sem("g_in"), [sem("w_stream0"), sem("w_stream1")], sem("pool_w_in"), sem("router_w_in")
        consts, zero_ready, rows_zeroed = sem("consts"), sem("zero_ready"), sem("rows_zeroed")
        toep_zero, taps_ready, taps_out, toep_in = sem("toep_zero"), sem("taps_ready"), sem("taps_out"), sem("toep_in")
        psum_ready = sem("psum_ready")
        emptied = {"act": sem("emptied_act"), "dve": sem("emptied_dve")}
        squares, mean_sq, root, xn_ready = sem("squares"), sem("mean_sq"), sem("root"), sem("xn_ready")
        step_dve, step_pool, ss_ready = sem("step_dve"), sem("step_pool"), sem("ss_ready")
        bbd_ready, cpow_ready, s_ready = sem("bbd_ready"), sem("cpow_ready"), sem("s_ready")
        hpad_zero, hpad_ready, scan_step, fin_ready = sem("hpad_zero"), sem("hpad_ready"), sem("scan_step"), sem("fin_ready")
        halo_ready, z_ready = sem("halo_ready"), sem("z_ready")
        gated, merged = sem("gated"), sem("merged")
        squares2, mean2, root2, xn2_ready = sem("squares2"), sem("mean2"), sem("root2"), sem("xn2_ready")
        neg_ready, exp_ready, chosen_ready, rows_ready = sem("neg_ready"), sem("exp_ready"), sem("chosen_ready"), sem("rows_ready")
        scattered, counts_ready = sem("scattered"), sem("counts_ready")
        outs_done = sem("outs_done")
        xg_in = [sem("xg_in0"), sem("xg_in1")]
        wg_in, wu_in, wd_in = ([sem(f"{n}_in{k}") for k in range(2)] for n in ("gate", "up", "down"))
        xt_done, gu_done, ht_done, dn_done = sem("xt_done"), sem("gate_up_done"), sem("ht_done"), sem("down_done")
        xgt_ready, silu_ready, h_ready, hT_ready, y_ready = sem("xgt_ready"), sem("silu_ready"), sem("h_ready"), sem("ht_ready"), sem("y_ready")
        y_stored = [sem("y_stored0"), sem("y_stored1")]
        ov_done, ov_x, ov_w, ov_pe, ov_act, ov_dve, ov_store = (sem(f"overflow_{n}") for n in ("done", "x", "w", "pe", "act", "dve", "store"))
        gathered = [sem(f"gathered{i}") for i in range(TT)]
        sum_ready, squares3, mean3, root3, final_ready = sem("sum_ready"), sem("squares3"), sem("mean3"), sem("root3"), sem("final_ready")

        def psum_waits(eng, name):
            eng.wait_ge(psum_ready, NUM[name] + 1)

        w_gate = a["w_exp_gate"][0].rearrange("e (k p) n -> e p k n", p=P)
        w_up = a["w_exp_up"][0].rearrange("e (k p) n -> e p k n", p=P)
        w_down = a["w_exp_down"][0].rearrange("e (k p) n -> e p k n", p=P)

        def expert_row(src, e):
            return src[bass.ds(e, 1)].rearrange("o p k n -> (o p) k n")

        def w_slot(s, k):
            return slot(s).rearrange("p (k n) -> p k n", k=k)

        def overflow(eng, body):
            any_extra = eng.value_load(table[0:1, 2 * NE * EXTRA:2 * NE * EXTRA + 1], min_val=0, max_val=1)
            count = eng.alloc_register()
            eng.reg_mov(count, 1)
            with eng.If(any_extra > 0):
                with eng.Fori(0, NE * EXTRA) as i:
                    used = eng.value_load(table[0:1, bass.ds(i, 1)], min_val=0, max_val=1)
                    with eng.If(used > 0):
                        e_row = eng.value_load(table[0:1, bass.ds(i + NE * EXTRA, 1)],
                                               min_val=0, max_val=NROWS - TILE)
                        body(i, e_row, eng.snap(count, min_val=1, max_val=NE * EXTRA + 1))
                        eng.reg_add(count, count, 1)

        block = ctx.enter_context(nc.Block())

        @block.sync
        def _(sp):
            for i in range(TT):
                src = a["x_prompt"][0, i * P:(i + 1) * P] if i < 4 else a["x_sample"][0]
                sp.dma_start(x_tok[:ROWS[i], i, :], src).then_inc(x_in, 16)
            w_in = a["w_in"][0].rearrange("(k p) (b n) -> b p k n", p=P, b=6)
            glu = [a[n][0].rearrange("(k p) n -> p k n", p=P) for n in ("w_glu_a", "w_glu_b")]
            w_out = a["w_out"][0].rearrange("(k p) (b n) -> b p k n", p=P, b=2)
            stream = [(w_in[0], 8, "u3"), (w_in[2], 8, "gs3"), (w_in[3], 8, "gs7"), (w_in[1], 8, "up3"),
                      (w_in[4], 8, "gp3"), (w_in[5], 8, "gp7"), (glu[0], 4, "ga7"), (glu[1], 4, "gb7"),
                      (w_out[0], 8, None), (w_out[1], 8, None)]
            for b, (src, k, _) in enumerate(stream):
                if b >= 2:
                    psum_waits(sp, stream[b - 2][2])
                if b == 7:
                    sp.dma_start(pool_w.rearrange("p (g n) -> p g n", g=4),
                                 a["pool_w"][0].rearrange("g p n -> p g n")).then_inc(pw_in, 16)
                sp.dma_start(w_slot(b % 2, k), src).then_inc(w_stream[b % 2], 16)
                if b == 5:
                    sp.wait_ge(emptied["dve"], emptied_by("dve", NUM["fin"]))
                    for n, name in enumerate(("re_p", "im_p", "re_s", "im_s")):
                        sp.dma_start(out[name].rearrange("a b (j g) n -> (a b j) (g n)", g=2),
                                     fin_rows[16 * n:16 * n + 16, :]).then_inc(outs_done, 16)
            sp.wait_ge(emptied["act"], emptied_by("act", NUM["hist"]))
            for n, name in enumerate(("hist_p", "hist_s")):
                sp.dma_start(out[name][0, 0], hist_rows[:, n * 512:n * 512 + 512]).then_inc(outs_done, 16)

            def load(e, par, first=False):
                if not first:
                    sp.wait_ge(xt_done, e - 1)
                sp.dma_start(xg[par], x_rows[bass.ds(e * TILE, TILE), :]).then_inc(xg_in[par], 16)
                if not first:
                    sp.wait_ge(gu_done, e - 1)
                sp.dma_start(w_slot(GATE[par], 8), expert_row(w_gate, e)).then_inc(wg_in[par], 16)
                sp.dma_start(w_slot(UP[par], 8), expert_row(w_up, e)).then_inc(wu_in[par], 16)
                if not first:
                    sp.wait_ge(dn_done, e - 1)
                sp.dma_start(w_slot(DOWN[par], 4), expert_row(w_down, e)).then_inc(wd_in[par], 16)

            psum_waits(sp, "gt3")
            sp.wait_ge(emptied["dve"], emptied_by("dve", NUM["gt3"]))
            sp.dma_start(w_slot(GATE[0], 8), w_gate[0]).then_inc(wg_in[0], 16)
            sp.dma_start(w_slot(UP[0], 8), w_up[0]).then_inc(wu_in[0], 16)
            sp.wait_ge(merged, 8)
            sp.dma_start(w_slot(DOWN[0], 4), w_down[0]).then_inc(wd_in[0], 16)
            sp.dma_start(w_slot(GATE[1], 8), w_gate[1]).then_inc(wg_in[1], 16)
            psum_waits(sp, "out4")
            sp.dma_start(w_slot(UP[1], 8), w_up[1]).then_inc(wu_in[1], 16)
            sp.dma_start(w_slot(DOWN[1], 4), w_down[1]).then_inc(wd_in[1], 16)
            sp.wait_ge(scattered, 16 * 2 * TT)
            for e in range(2):
                sp.dma_start(xg[e], x_rows[e * TILE:(e + 1) * TILE, :]).then_inc(xg_in[e], 16)
            with sp.Fori(1, NE // 2) as i:
                for par in range(2):
                    load(2 * i + par, par)

            sp.wait_ge(counts_ready, 1)

            def more(i, row, n):
                sp.wait_ge(ov_done, n)
                sp.dma_start(xg[0], x_rows[bass.ds(row, TILE), :]).then_inc(ov_x, 16)
                e = i // EXTRA
                sp.dma_start(w_slot(GATE[0], 8), expert_row(w_gate, e)).then_inc(ov_w, 16)
                sp.dma_start(w_slot(UP[0], 8), expert_row(w_up, e)).then_inc(ov_w, 16)
                sp.dma_start(w_slot(DOWN[0], 4), expert_row(w_down, e)).then_inc(ov_w, 16)

            overflow(sp, more)
            for i in range(TT):
                sp.wait_ge(final_ready, i + 1)
                dst = out["y_prompt"][0, i * P:(i + 1) * P] if i < 4 else out["y_sample"][0]
                sp.dma_start(dst, xn2[:ROWS[i], i, :]).then_inc(outs_done, 16)
            sp.wait_ge(outs_done, 16 * (4 + 2 + TT))

        @block.gpsimd
        def _(pool):
            done = [0]

            def step(ins):
                done[0] += 1
                ins.then_inc(step_pool, 1)
                pool.wait_ge(step_pool, done[0])

            step(pool.memset(ident, 0.0))
            pool.affine_select(out=ident, in_=ident, compare_op=ALU.not_equal, fill=1.0, base=0,
                               pattern=[[-1, P]], channel_multiplier=1).then_inc(consts, 1)
            step(pool.memset(diag16, 0.0))
            for g in range(8):
                step(pool.affine_select(out=diag16, in_=diag16, compare_op=ALU.not_equal, fill=1.0, base=-16 * g,
                                        pattern=[[-1, 16]], channel_multiplier=1))
            step(pool.memset(tri, 1.0))
            pool.memset(ones, 1.0)
            step(pool.affine_select(out=tri, in_=tri, compare_op=ALU.is_gt, fill=0.0, base=0,
                                    pattern=[[1, P]], channel_multiplier=-1))
            for gi, w in enumerate(WINDOWS):
                for c in range(HIST):
                    pool.memset(inv[:, gi, c:c + 1], 1.0 / min(w, c + 1))
            pool.iota(ebase, pattern=[[TILE, NE]], base=0, channel_multiplier=0,
                      allow_small_or_imprecise_dtypes=True).then_inc(consts, 1)
            pool.memset(zeros, 0.0).then_inc(zero_ready, 1)
            pool.memset(bbd, 0.0).then_inc(toep_zero, 1)
            pool.memset(toep, 0.0).then_inc(toep_zero, 1)
            pool.wait_ge(zero_ready, 1)
            with pool.Fori(0, NROWS // P) as n:
                pool.dma_start(x_rows[bass.ds(n * P, P), :], zeros).then_inc(rows_zeroed, 16)
            with pool.Fori(MAIN // P, NROWS // P) as n:
                pool.dma_start(y_rows[bass.ds(n * P, P), :], zeros).then_inc(rows_zeroed, 16)
            pool.wait_ge(taps_ready, 4)
            pool.dma_start(kd, k_sb).then_inc(taps_out, 16)
            pool.wait_ge(taps_out, 16)
            pool.wait_ge(toep_zero, 2)
            taps = kd.rearrange("(g q) (b n) -> q b g n", q=Q, b=4)
            for s in range(L):
                dst = toep[16 * s:16 * s + 16].rearrange("q (b g n) -> q b g n", b=4, g=8)
                for b in range(4):
                    pool.dma_start(dst[:, b, :, 16 * s:P], taps[:, b, :, 0:P - 16 * s]).then_inc(toep_in, 16)
            psum_waits(pool, "usq3")
            pool.memset(at(O_HPAD, NJ * 4 * NC), 0.0).then_inc(hpad_zero, 1)
            psum_waits(pool, "y3")
            pool.memset(up_t[:, :, 0:HIST], 0.0).then_inc(halo_ready, 1)
            pool.tensor_copy(up_t[:, :, HIST + SEQ:2 * HIST + SEQ], hist_t).then_inc(halo_ready, 1)
            psum_waits(pool, "fin")
            for gi, w in enumerate(WINDOWS):
                pool.wait_ge(emptied["act"], emptied_by("act", NUM[f"up{gi}"]))
                pool.wait_ge(halo_ready, 2)
                src, span, n = up_t[:, gi, :], 1, 0
                while span < w:
                    dst = win[n % 2]
                    step(pool.tensor_tensor(dst[:, 2 * span - 1:UPW], src[:, 2 * span - 1:UPW],
                                            src[:, span - 1:UPW - span], ALU.add))
                    src, span, n = dst, 2 * span, n + 1
                z = z_t[:, gi, :]
                step(pool.tensor_scalar(z[:, 0:SEQ], src[:, HIST:HIST + SEQ], 1.0 / w, None, ALU.mult))
                step(pool.tensor_tensor(z[:, 0:HIST], src[:, HIST:2 * HIST], inv[:, gi, :], ALU.mult))
                step(pool.tensor_scalar(z[:, SEQ:NT], src[:, 2 * HIST + SEQ:UPW], 1.0 / w, None, ALU.mult))
                step(pool.tensor_tensor(z[:, 0:SEQ], z[:, 0:SEQ], up_t[:, gi, HIST:HIST + SEQ], ALU.subtract))
                pool.tensor_tensor(z[:, SEQ:NT], z[:, SEQ:NT], up_t[:, gi, 2 * HIST + SEQ:UPW],
                                   ALU.subtract).then_inc(z_ready, 1)
            for m in range(8):
                pool.wait_ge(emptied["dve"], emptied_by("dve", NUM[f"ga{m}"]))
                pool.tensor_tensor(t1[m % 2], t1[m % 2], sgs[:, m, :], ALU.mult).then_inc(gated, 1)
                pool.wait_ge(gated, m + 1)
                pool.wait_ge(emptied["dve"], emptied_by("dve", NUM[f"po{m}"]))
                pool.tensor_tensor(m_t[:, m, :], t1[m % 2], t2[m % 2], ALU.add).then_inc(merged, 1)
            pool.wait_ge(rows_zeroed, 16 * ZEROED)
            pool.wait_ge(rows_ready, 1)
            for i in range(TT):
                for k in range(2):
                    pool.indirect_dma_start(
                        out=x_rows, out_offset=bass.IndirectOffsetOnAxis(ap=rows_i[:ROWS[i], i, k:k + 1], axis=0),
                        in_=xn2[:ROWS[i], i, :], in_offset=None).then_inc(scattered, 16)

            def store(e, par):
                pool.wait_ge(y_ready, e + 1)
                pool.dma_start(y_rows[bass.ds(e * TILE, TILE), :], y_sb[par]).then_inc(y_stored[par], 16)

            with pool.Fori(0, NE // 2) as i:
                for par in range(2):
                    store(2 * i + par, par)
            for par in range(2):
                pool.wait_ge(y_stored[par], 16 * (NE // 2))
            pool.wait_ge(counts_ready, 1)
            pool.sem_inc(ov_done, 1)

            def more(i, row, n):
                pool.wait_ge(ov_dve, n * 3)
                pool.dma_start(y_rows[bass.ds(row, TILE), :], y_sb[0]).then_inc(ov_store, 16)
                pool.wait_ge(ov_store, n * 16)
                pool.sem_inc(ov_done, 1)

            overflow(pool, more)
            for i in range(TT):
                for k in range(2):
                    pool.indirect_dma_start(
                        out=at((2 * i + k) * D, D, ROWS[i]), out_offset=None, in_=y_rows,
                        in_offset=bass.IndirectOffsetOnAxis(ap=rows_i[:ROWS[i], i, k:k + 1], axis=0),
                    ).then_inc(gathered[i], 16)

        @block.scalar
        def _(act):
            def load(dst, src, s):
                act.dma_start(dst, src).then_inc(s, 16)

            def emptying(ins):
                ins.then_inc(emptied["act"], 1)

            load(g_b, a["g_mix"][0:1].to_broadcast((P, D)), g_in)
            par_dst = [(0, "ssm_a_re"), (16, "ssm_a_im"), (32, "state_ssm_re"), (48, "state_ssm_im")]
            for r, name in par_dst:
                src = a[name][0] if name[:3] == "ssm" else a[name][0, 0]
                load(par_rows[r:r + 16, :], src.rearrange("(j g) n -> j (g n)", g=2), small_in)
            load(dt_rows, a["ssm_log_dt"][0].rearrange("(j g) -> j g", g=2), small_in)
            load(par_rows[80:84, :], a["ssm_d"][0].rearrange("(b g) q -> b (g q)", b=4), small_in)
            load(par_rows[84:92, :], a["pool_scale"][0].rearrange("(m p) -> m p", p=P), small_in)
            load(cache_rows, a["cache_pool"][0, 0], small_in)
            for r, name in enumerate(("ssm_b_re", "ssm_b_im")):
                load(b_in[:, r], a[name][0].rearrange("(j g) n q -> (g n) j q", g=2), b_loaded)
            for r, name in enumerate(("ssm_c_re", "ssm_c_im")):
                src = a[name][0].rearrange("(h j g) q n -> g h j q n", h=2, g=2)
                dst = c_in.rearrange("p (r h g n) -> p r h g n", r=2, h=2, g=2)
                for hh in range(2):
                    for g in range(2):
                        load(dst[:, r, hh, g, :], src[g, hh], c_loaded)
            load(w_r[:, :, 0:4], a["w_router_group"][0].rearrange("(k p) n -> p k n", p=P), wr_in)
            load(w_r[:, :, 4:36], a["w_router_expert"][0].rearrange("(k p) g e -> p k (g e)", p=P), wr_in)
            act.wait_ge(ss_ready, 1)
            act.wait_ge(x_in, 16 * TT)
            for i in range(TT):
                if i:
                    act.wait_ge(squares, i)
                act.activation(junk0[:ROWS[i]], x_tok[:ROWS[i], i, :], ACT.Square,
                               accum_out=ss[:ROWS[i], i:i + 1]).then_inc(squares, 1)
            act.wait_ge(mean_sq, 1)
            act.activation(rstd, ss, ACT.Sqrt).then_inc(root, 1)
            for i in range(TT):
                psum_waits(act, f"xt{i}")
                r = ROWS[i]
                src = pair(NUM[f"xt{i}"]).rearrange("p h (k t) -> p (h k) t", k=4)
                emptying(act.activation(xn_t[:, :, i * P:i * P + r], src[:, :, 0:r], ACT.Copy))

            def halves(ap):
                return ap.rearrange("p (h t) -> p h t", h=2)

            def evacuate(name, dst, func):
                psum_waits(act, name)
                emptying(act.activation(halves(dst), pair(NUM[name])[:, :, 0:HALF], func))

            for m in range(4):
                evacuate(f"u{m}", u_t[:, m, :], ACT.Copy)
            for m in range(4):
                evacuate(f"gs{m}", sgs[:, m, :], ACT.Sigmoid)
            for r in range(4):
                psum_waits(act, f"st{r}")
                emptying(act.activation(s_t[:, r * 1024:(r + 1) * 1024].rearrange("p (h n) -> p h n", h=2),
                                        pair(NUM[f"st{r}"]), ACT.Copy))
            for r in range(4):
                psum_waits(act, f"usq{r}")
                emptying(act.activation(usq[:, r * 8 * NC:(r + 1) * 8 * NC].rearrange("p (h n) -> p h n", h=2),
                                        pair(NUM[f"usq{r}"])[:, :, 0:4 * NC], ACT.Copy))
            for m in range(4, 8):
                evacuate(f"gs{m}", sgs[:, m, :], ACT.Sigmoid)
            for r in range(4):
                psum_waits(act, f"y{r}")
                dst = gc[0:NC].rearrange("c (t b g q) -> c b g t q", t=L, b=4, g=8)[:, r]
                src = pair(NUM[f"y{r}"])[0:NC].rearrange("c h (g t q) -> c (h g) t q", g=4, t=L)
                emptying(act.activation(dst, src, ACT.Gelu_apprx_tanh))
            for m in range(4):
                psum_waits(act, f"up{m}")
                src = pair(NUM[f"up{m}"])
                act.activation(up_t[:, m, HIST:HIST + HALF], src[:, 0, 0:HALF], ACT.Copy)
                act.activation(up_t[:, m, HIST + HALF:HIST + SEQ], src[:, 1, 0:SEQ - HALF], ACT.Copy)
                emptying(act.activation(up_t[:, m, 2 * HIST + SEQ:UPW], src[:, 1, SEQ - HALF:HALF], ACT.Copy))
            psum_waits(act, "hist")
            emptying(act.activation(hist_rows.rearrange("p (s n) -> p s n", s=2), pair(NUM["hist"])[0:HIST], ACT.Copy))
            psum_waits(act, "gt3")
            for m in range(8):
                evacuate(f"gp{m}", sgp[:, m, :], ACT.Sigmoid)
            for m in range(8):
                psum_waits(act, f"gb{m}")
                if m >= 2:
                    act.wait_ge(emptied["dve"], emptied_by("dve", NUM[f"ga{m - 2}"]))
                act.activation(halves(sig_b[m % 2]), pair(NUM[f"gb{m}"])[:, :, 0:HALF], ACT.Sigmoid)\
                    .then_inc(emptied["act"], 1)
            act.wait_ge(xn_ready, TT)
            load(g_b, a["g_ffn"][0:1].to_broadcast((P, D)), g_in)

            def norm2(i):
                act.wait_ge(emptied["dve"], emptied_by("dve", NUM[f"out{i}"]))
                if i:
                    act.wait_ge(squares2, i)
                act.activation(junk1[:ROWS[i]], x_tok[:ROWS[i], i, :], ACT.Square,
                               accum_out=ss[:ROWS[i], i:i + 1]).then_inc(squares2, 1)
                act.wait_ge(mean2, i + 1)
                act.activation(rstd[:ROWS[i], i:i + 1], ss[:ROWS[i], i:i + 1], ACT.Sqrt).then_inc(root2, 1)

            def x2t(i):
                psum_waits(act, f"x2t{i}")
                r = ROWS[i]
                src = pair(NUM[f"x2t{i}"]).rearrange("p h (k t) -> p (h k) t", k=4)
                emptying(act.activation(xn2_t[:, :, i * P:i * P + r], src[:, :, 0:r], ACT.Copy))

            norm2(0)
            for i in range(TT):
                if i + 1 < TT:
                    norm2(i + 1)
                x2t(i)
            act.wait_ge(xn2_ready, TT)
            load(g_b, a["g_final"].rearrange("(o d) -> o d", o=1).to_broadcast((P, D)), g_in)
            act.wait_ge(neg_ready, 1)
            act.activation(g_exp, g_exp, ACT.Exp).then_inc(exp_ready, 1)
            act.wait_ge(neg_ready, 2)
            act.activation(e_neg, e_neg, ACT.Exp).then_inc(exp_ready, 1)

            def copy_xt(e, par):
                act.wait_ge(xt_done, e + 1)
                act.activation(xg_t[par].rearrange("p (h n) -> p h n", h=2),
                               ps[:, 0:2, 0:4 * TILE], ACT.Copy).then_inc(xgt_ready, 1)

            def gate(e, par, early):
                act.wait_ge(gu_done, e + 1)
                if not early:
                    act.wait_ge(h_ready, e - 1)
                act.activation(silu[par], ps[0:TILE, 2, :], ACT.Silu).then_inc(silu_ready, 1)

            copy_xt(0, 0)
            for e in range(2):
                gate(e, e, True)
                copy_xt(e + 1, (e + 1) % 2)
            with act.Fori(1, NE // 2 - 1) as i:
                for par in range(2):
                    gate(2 * i + par, par, False)
                    copy_xt(2 * i + par + 1, 1 - par)
            gate(NE - 2, 0, False)
            copy_xt(NE - 1, 1)
            gate(NE - 1, 1, False)
            act.wait_ge(counts_ready, 1)

            def more(i, row, n):
                act.wait_ge(ov_pe, n * 4 - 3)
                act.activation(xg_t[0].rearrange("p (h n) -> p h n", h=2),
                               ps[:, 0:2, 0:4 * TILE], ACT.Copy).then_inc(ov_act, 1)
                act.wait_ge(ov_pe, n * 4 - 2)
                act.activation(silu[0], ps[0:TILE, 2, :], ACT.Silu).then_inc(ov_act, 1)

            overflow(act, more)
            for i in range(TT):
                act.wait_ge(sum_ready, i + 1)
                act.activation(at(10 * D + i * D, D, ROWS[i]), x_tok[:ROWS[i], i, :], ACT.Square,
                               accum_out=ss[:ROWS[i], i:i + 1]).then_inc(squares3, 1)
                act.wait_ge(mean3, i + 1)
                act.activation(rstd[:ROWS[i], i:i + 1], ss[:ROWS[i], i:i + 1], ACT.Sqrt).then_inc(root3, 1)

        @block.vector
        def _(dve):
            done = [0]

            def step(ins):
                done[0] += 1
                ins.then_inc(step_dve, 1)
                dve.wait_ge(step_dve, done[0])

            def tt(out_, x0, x1, op):
                step(dve.tensor_tensor(out_, x0, x1, op))

            def ts(out_, x0, s0, op0, s1=None, op1=None):
                if op1 is None:
                    step(dve.tensor_scalar(out_, x0, s0, None, op0))
                else:
                    step(dve.tensor_scalar(out_, x0, s0, s1, op0, op1))

            def stt(out_, x0, s0, x1, op0, op1):
                step(dve.scalar_tensor_tensor(out=out_, in0=x0, scalar=s0, in1=x1, op0=op0, op1=op1))

            def inverse_root(mean, r):
                tmp = misc(M_SS + 16, TT)[0:r.shape[0], 0:r.shape[1]]
                step(dve.reciprocal(r, r))
                tt(tmp, r, r, ALU.mult)
                tt(tmp, tmp, mean, ALU.mult)
                ts(tmp, tmp, -0.5, ALU.mult, 1.5, ALU.add)
                tt(r, r, tmp, ALU.mult)

            taken = [0]

            def empty(ins, read=False):
                taken[0] += 1
                ins.then_inc(emptied["dve"], 1)
                if read:
                    dve.wait_ge(emptied["dve"], taken[0])

            step(dve.memset(ss, 1.0))
            dve.memset(rstd, 1.0).then_inc(ss_ready, 1)
            dve.wait_ge(small_in, 16 * 8)
            for g in range(2):
                dve.tensor_copy(par_rows[64:80, g * N:(g + 1) * N],
                                dt_rows[:, g:g + 1].to_broadcast((NJ, N))).then_inc(dt_ready, 1)
            dve.wait_ge(squares, TT)
            dve.tensor_scalar(ss, ss, 1.0 / D, EPS, ALU.mult, ALU.add).then_inc(mean_sq, 1)
            dve.wait_ge(mean_sq, 1)
            dve.wait_ge(root, 1)
            inverse_root(ss, rstd)
            dve.wait_ge(g_in, 16)
            for i in range(TT):
                if i >= 2:
                    psum_waits(dve, f"xt{i - 2}")
                r = ROWS[i]
                dve.scalar_tensor_tensor(out=xn_row[i % 2][:r], in0=x_tok[:r, i, :], scalar=rstd[:r, i:i + 1],
                                         in1=g_b[:r], op0=ALU.mult, op1=ALU.mult).then_inc(xn_ready, 1)

            psum_waits(dve, "par")
            pp = pair(NUM["par"])
            step(dve.tensor_copy(prm, pp[:, 0, 0:92]))
            step(dve.tensor_copy(hist_t.rearrange("p g c -> p (g c)"), pp[:, 0, 128:188]))
            empty(dve.tensor_copy(c_t.rearrange("p r j q -> p (r j q)"), pp[:, 1, :]), read=True)
            col = lambda n: misc(M_TMP + 16 * n, 16)
            a_re, a_im, log_dt, d_col = prm[:, 0:16], prm[:, 16:32], prm[:, 64:80], prm[:, 80:84]

            def exp(dst, z, k, r, ki):
                ts(dst, z, 87.0, ALU.min, -87.0, ALU.max)
                ts(k, dst, 1.4426950408889634, ALU.mult, 12582912.0, ALU.add)
                ts(k, k, -12582912.0, ALU.add)
                stt(r, k, -0.693145751953125, dst, ALU.mult, ALU.add)
                stt(r, k, -1.42860677e-06, r, ALU.mult, ALU.add)
                ts(k, k, 127.0, ALU.add)
                step(dve.tensor_copy(ki.bitcast(I32), k))
                ts(ki.bitcast(I32), ki.bitcast(I32), 23, ALU.logical_shift_left)
                ts(dst, r, 1.0 / 5040, ALU.mult)
                for c in (1.0 / 720, 1.0 / 120, 1.0 / 24, 1.0 / 6, 0.5, 1.0):
                    stt(dst, dst, c, r, ALU.add, ALU.mult)
                ts(dst, dst, 1.0, ALU.add)
                tt(dst, dst, ki, ALU.mult)

            dt, lr, mag, ang, s1, s2 = col(0), col(1), col(2), col(3), col(4), col(5)
            t_a, t_b, t_c = col(6), col(7), col(8)
            exp(dt, log_dt, t_a, t_b, t_c)
            ts(lr, a_re, -1e-4, ALU.min)
            tt(s1, lr, dt, ALU.mult)
            exp(mag, s1, t_a, t_b, t_c)
            tt(ang, a_im, dt, ALU.mult)
            ts(t_a, ang, 0.15915494309189535, ALU.mult, 12582912.0, ALU.add)
            ts(t_a, t_a, -12582912.0, ALU.add)
            for c in (6.28125, 0.0019340515136718750, 1.2556659146547282e-06):
                stt(ang, t_a, -c, ang, ALU.mult, ALU.add)
            ts(ang, ang, 0.5, ALU.mult)
            tt(t_a, ang, ang, ALU.mult)
            sin_c = (-1.0 / 39916800, 1.0 / 362880, -1.0 / 5040, 1.0 / 120, -1.0 / 6)
            ts(s1, t_a, 1.0 / 6227020800, ALU.mult)
            for c in sin_c:
                stt(s1, s1, c, t_a, ALU.add, ALU.mult)
            stt(s1, s1, 1.0, ang, ALU.add, ALU.mult)
            cos_c = (1.0 / 479001600, -1.0 / 3628800, 1.0 / 40320, -1.0 / 720, 1.0 / 24, -0.5)
            ts(s2, t_a, -1.0 / 87178291200, ALU.mult)
            for c in cos_c:
                stt(s2, s2, c, t_a, ALU.add, ALU.mult)
            ts(s2, s2, 1.0, ALU.add)
            tt(t_b, s1, s2, ALU.mult)
            stt(t_b, t_b, 2.0, mag, ALU.mult, ALU.mult)
            tt(t_a, s1, s1, ALU.mult)
            ts(t_a, t_a, -2.0, ALU.mult, 1.0, ALU.add)
            tt(t_a, t_a, mag, ALU.mult)
            pre, pim = powers[:, 0], powers[:, 1]
            step(dve.memset(pre[:, 0], 1.0))
            step(dve.memset(pim[:, 0], 0.0))
            step(dve.tensor_copy(pre[:, 1], t_a))
            step(dve.tensor_copy(pim[:, 1], t_b))

            def cmul(dr, di, ar, ai, br, bi, t, ready=None):
                tt(dr, ar, br, ALU.mult)
                tt(t, ai, bi, ALU.mult)
                tt(dr, dr, t, ALU.subtract)
                tt(di, ar, bi, ALU.mult)
                tt(t, ai, br, ALU.mult)
                if ready is None:
                    tt(di, di, t, ALU.add)
                else:
                    dve.tensor_tensor(di, di, t, ALU.add).then_inc(ready, 1)

            for k in (1, 2, 4):
                shape = (P, k, NJ)
                tmp = misc(M_TMP + 320, k * NJ).rearrange("p (t j) -> p t j", t=k)
                cmul(pre[:, k + 1:2 * k + 1], pim[:, k + 1:2 * k + 1], pre[:, 1:k + 1], pim[:, 1:k + 1],
                     pre[:, k:k + 1].to_broadcast(shape), pim[:, k:k + 1].to_broadcast(shape), tmp)
            step(dve.tensor_copy(a4[:, :, 0, 0], pre[:, 8]))
            step(dve.tensor_copy(a4[:, :, 1, 1], pre[:, 8]))
            step(dve.tensor_copy(a4[:, :, 1, 0], pim[:, 8]))
            ts(a4[:, :, 0, 1], pim[:, 8], -1.0, ALU.mult)
            num, den, k_re, k_im = col(9), col(10), col(11), col(12)
            ts(num, t_a, -1.0, ALU.add)
            tt(den, lr, lr, ALU.mult)
            tt(s1, a_im, a_im, ALU.mult)
            tt(den, den, s1, ALU.add)
            step(dve.reciprocal(den, den))
            tt(k_re, num, lr, ALU.mult)
            tt(s1, t_b, a_im, ALU.mult)
            tt(k_re, k_re, s1, ALU.add)
            tt(k_re, k_re, den, ALU.mult)
            tt(k_im, t_b, lr, ALU.mult)
            tt(s1, num, a_im, ALU.mult)
            tt(k_im, k_im, s1, ALU.subtract)
            tt(k_im, k_im, den, ALU.mult)
            dve.wait_ge(b_loaded, 32)
            wide = (P, NJ, Q)
            tmp = prod[:, 0:256].rearrange("p (j q) -> p j q", j=NJ)
            cmul(bbar[:, 0], bbar[:, 1], k_re.unsqueeze(2).to_broadcast(wide), k_im.unsqueeze(2).to_broadcast(wide),
                 b_in[:, 0], b_in[:, 1], tmp)
            dve.wait_ge(toep_zero, 1)
            bb = bbd.rearrange("p (j r g q) -> p r j g q", j=NJ, r=2, g=2)
            for r in range(2):
                for g in range(2):
                    dve.tensor_copy(bb[64 * g:64 * g + 64, r, :, g, :], bbar[64 * g:64 * g + 64, r])\
                        .then_inc(bbd_ready, 1)
            big = (P, NJ, 9, Q)
            cp = [c.rearrange("p (j t q) -> p j t q", j=NJ, t=9) for c in cpow]
            tmp = prod.rearrange("p (j t q) -> p j t q", j=NJ, t=9)
            c_b = [c_t[:, r].unsqueeze(2).to_broadcast(big) for r in range(2)]
            p_b = [x.rearrange("p t j -> p j t").unsqueeze(3).to_broadcast(big) for x in (pre, pim)]
            tt(cp[0], c_b[0], p_b[0], ALU.mult)
            tt(tmp, c_b[1], p_b[1], ALU.mult)
            tt(cp[0], cp[0], tmp, ALU.subtract)
            tt(cp[1], c_b[0], p_b[1], ALU.mult)
            tt(tmp, c_b[1], p_b[0], ALU.mult)
            dve.scalar_tensor_tensor(out=cp[1], in0=cp[1], scalar=-1.0, in1=tmp, op0=ALU.mult, op1=ALU.subtract)\
                .then_inc(cpow_ready, 1)
            sn = s_nat.rearrange("p (j r s q) -> p r s j q", j=NJ, r=2, s=L)
            tmp = prod[:, 0:256].rearrange("p (j q) -> p j q", j=NJ)
            for s in range(L):
                p_re = pre[:, 7 - s].unsqueeze(2).to_broadcast(wide)
                p_im = pim[:, 7 - s].unsqueeze(2).to_broadcast(wide)
                cmul(sn[:, 0, s], sn[:, 1, s], p_re, p_im, bbar[:, 0], bbar[:, 1], tmp,
                     s_ready if s == L - 1 else None)

            psum_waits(dve, "kt")
            empty(dve.tensor_copy(k_sb, pair(NUM["kt"])[:, 0, :]), read=True)
            for b in range(4):
                lag0 = k_sb[:, b * P:b * P + Q]
                dve.scalar_tensor_tensor(out=lag0, in0=diag16, scalar=d_col[:, b:b + 1], in1=lag0,
                                         op0=ALU.mult, op1=ALU.add).then_inc(taps_ready, 1)
            dve.wait_ge(rows_zeroed, 16 * ZEROED)
            for r in range(4):
                psum_waits(dve, f"uc{r}")
                empty(dve.tensor_copy(uc[0:NC].rearrange("c (g s q) -> c s g q", s=L, g=G)[:, 2 * r:2 * r + 2],
                                      pair(NUM[f"uc{r}"])[0:NC].rearrange("c h (g q) -> c h g q", g=G)))
            dve.wait_ge(taps_out, 16)
            for r in range(3):
                psum_waits(dve, f"v{r}")
                for b in range(2):
                    n = min(3, NJ - (6 * r + 3 * b))
                    copied = dve.tensor_copy(v_all[:, (6 * r + 3 * b) * 2 * NC:(6 * r + 3 * b + n) * 2 * NC],
                                             pair(NUM[f"v{r}"])[:, b, 0:n * 2 * NC])
                    if b == 0:
                        step(copied)
                    else:
                        empty(copied, read=True)
            four = (P, NJ, 2, 2)

            def before_sample():
                return prm[:, 32:64].rearrange("p (r j) -> p j r", r=2)

            def advance(state, c):
                tt(scan_tmp, a4, state.unsqueeze(2).to_broadcast(four), ALU.mult)
                step(dve.tensor_reduce(scan_red, scan_tmp, X, ALU.add))
                tt(v[:, :, :, c], v[:, :, :, c], scan_red, ALU.add)

            advance(before_sample(), PC)
            for c in range(PC + 1, NC):
                advance(v[:, :, :, c - 1], c)
            with dve.Fori(1, PC) as c:
                prev = v[:, :, :, bass.ds(c - 1, 1)].rearrange("p j r c -> p j (r c)")
                here = v[:, :, :, bass.ds(c, 1)].rearrange("p j r c -> p j (r c)")
                dve.tensor_tensor(scan_tmp, a4, prev.unsqueeze(2).to_broadcast(four), ALU.mult).then_inc(scan_step, 1)
                dve.wait_ge(scan_step, c * 3 - 2)
                dve.tensor_reduce(scan_red, scan_tmp, X, ALU.add).then_inc(scan_step, 1)
                dve.wait_ge(scan_step, c * 3 - 1)
                dve.tensor_tensor(here, here, scan_red, ALU.add).then_inc(scan_step, 1)
                dve.wait_ge(scan_step, c * 3)
            dve.wait_ge(hpad_zero, 1)
            for g in range(2):
                row = slice(64 * g, 64 * g + 64)
                dve.tensor_copy(hpad[row, :, :, g, 1:PC], v[row, :, :, 0:PC - 1]).then_inc(hpad_ready, 1)
                dve.tensor_copy(hpad[row, :, :, g, PC], before_sample()[row]).then_inc(hpad_ready, 1)
                dve.tensor_copy(hpad[row, :, :, g, PC + 1:NC], v[row, :, :, PC:NC - 1]).then_inc(hpad_ready, 1)
            fc = fin_cols.rearrange("p (s r j) -> p s j r", s=2, r=2)
            dve.tensor_copy(fc[:, 0], v[:, :, :, PC - 1]).then_inc(fin_ready, 1)
            dve.tensor_copy(fc[:, 1], v[:, :, :, NC - 1]).then_inc(fin_ready, 1)
            for b in range(4):
                psum_waits(dve, f"gt{b}")
                dst = g_t[:, b, :].rearrange("p (c t) -> p t c", t=L)
                src = pair(NUM[f"gt{b}"])
                dve.tensor_copy(dst[:, 0:4], src[:, 0, 0:4 * NC].rearrange("p (t c) -> p t c", t=4))
                empty(dve.tensor_copy(dst[:, 4:8], src[:, 1, 0:4 * NC].rearrange("p (t c) -> p t c", t=4)))
            psum_waits(dve, "fin")
            empty(dve.tensor_copy(fin_rows, pair(NUM["fin"])[0:64, 0, 0:P]))

            def halves(ap):
                return ap.rearrange("p (h t) -> p h t", h=2)

            for m in range(8):
                psum_waits(dve, f"ga{m}")
                dve.wait_ge(emptied["act"], emptied_by("act", NUM[f"gb{m}"]))
                if m >= 2:
                    dve.wait_ge(merged, m - 1)
                empty(dve.tensor_tensor(halves(t1[m % 2]), pair(NUM[f"ga{m}"])[:, :, 0:HALF], halves(sig_b[m % 2]),
                                        ALU.mult))
                psum_waits(dve, f"po{m}")
                empty(dve.scalar_tensor_tensor(out=halves(t2[m % 2]), in0=pair(NUM[f"po{m}"])[:, :, 0:HALF],
                                               scalar=prm[:, 84 + m:85 + m], in1=halves(sgp[:, m, :]),
                                               op0=ALU.mult, op1=ALU.mult))
            for i in range(TT):
                psum_waits(dve, f"out{i}")
                r = ROWS[i]
                x_i = x_tok[:r, i, :].rearrange("p (h n) -> p h n", h=2)
                empty(dve.tensor_tensor(x_i, pair(NUM[f"out{i}"])[:r], x_i, ALU.add), read=True)
                dve.wait_ge(squares2, i + 1)
                mean, root_i = ss[:r, i:i + 1], rstd[:r, i:i + 1]
                dve.tensor_scalar(mean, mean, 1.0 / D, EPS, ALU.mult, ALU.add).then_inc(mean2, 1)
                dve.wait_ge(mean2, i + 1)
                dve.wait_ge(root2, i + 1)
                inverse_root(mean, root_i)
                dve.wait_ge(g_in, 32)
                dve.scalar_tensor_tensor(out=xn2[:r, i, :], in0=x_tok[:r, i, :], scalar=root_i, in1=g_b[:r],
                                         op0=ALU.mult, op1=ALU.mult).then_inc(xn2_ready, 1)
            dve.wait_ge(outs_done, 16 * 6)
            step(dve.memset(logits, 0.0))
            step(dve.tensor_copy(prefer, misc(M_EB, 8)))
            ts(prefer, prefer, -1.0 / TILE, ALU.mult, float(EI), ALU.add)
            psum_waits(dve, "lg")
            lg_ps = pair(NUM["lg"])[:, 0, 0:TT * 36].rearrange("p (i n) -> p i n", i=TT)
            step(dve.tensor_copy(logits[:, 0:4], lg_ps[:, 0:4]))
            empty(dve.tensor_copy(logits[:32, 4], lg_ps[:32, 4]), read=True)
            lg, le = logits[:, :, 0:EG], logits[:, :, EG:36]

            def first_max(hot, vals, best, rank, n):
                full = (P, TT, n)
                step(dve.tensor_reduce(best, vals, X, ALU.max))
                tt(hot, vals, best.unsqueeze(2).to_broadcast(full), ALU.is_equal)
                tt(hot, hot, rank.unsqueeze(1).to_broadcast(full), ALU.mult)
                step(dve.tensor_reduce(s_d, hot, X, ALU.max))
                tt(hot, hot, s_d.unsqueeze(2).to_broadcast(full), ALU.is_equal)

            first_max(g_hot, lg, s_a, prefer[:, 0:EG], EG)
            dve.tensor_tensor(g_exp, lg, s_a.unsqueeze(2).to_broadcast((P, TT, EG)), ALU.subtract)\
                .then_inc(neg_ready, 1)
            tt(le_mul, le.rearrange("p i (g e) -> p i g e", g=EG), g_hot.unsqueeze(3).to_broadcast((P, TT, EG, EI)),
               ALU.mult)
            step(dve.tensor_reduce(le_sel, le_mul.rearrange("p i g e -> p i e g"), X, ALU.add))
            first_max(i_hot[0], le_sel, s_b, prefer, EI)
            stt(i_tmp, i_hot[0], -BIG, le_sel, ALU.mult, ALU.add)
            first_max(i_hot[1], i_tmp, s_c, prefer, EI)
            dve.tensor_tensor(e_neg, s_c, s_b, ALU.subtract).then_inc(neg_ready, 1)
            for k in range(2):
                hot = onehot[k].rearrange("p i (g e) -> p i g e", g=EG)
                tt(hot, g_hot.unsqueeze(3).to_broadcast((P, TT, EG, EI)),
                   i_hot[k].unsqueeze(2).to_broadcast((P, TT, EG, EI)), ALU.mult)
            dve.tensor_tensor(chosen, onehot[0], onehot[1], ALU.add).then_inc(chosen_ready, 1)
            dve.wait_ge(exp_ready, 2)
            step(dve.tensor_reduce(s_a, g_exp, X, ALU.add))
            ts(s_b, e_neg, 1.0, ALU.add)
            tt(s_a, s_a, s_b, ALU.mult)
            step(dve.reciprocal(weight[:, :, 0], s_a))
            tt(weight[:, :, 1], weight[:, :, 0], e_neg, ALU.mult)
            psum_waits(dve, "rank")
            rk = pair(NUM["rank"])
            step(dve.tensor_copy(ranks[:, 0:4], rk[:, 0, 0:4 * NE].rearrange("p (i n) -> p i n", i=4)))
            step(dve.memset(rows_f, 0.0))
            step(dve.memset(ranks[:, 4], 0.0))
            step(dve.tensor_copy(ranks[:32, 4], rk[:32, 0, 4 * NE:5 * NE]))
            empty(dve.tensor_copy(counts, rk[:, 1, 0:NE]), read=True)
            full = (P, TT, NE)
            beyond, first = small(NE), [small(NE), small(NE)]
            ts(beyond, counts, -float(TILE), ALU.add, 0.0, ALU.max)
            step(dve.memset(first[0][:, 0:1], 0.0))
            step(dve.tensor_copy(first[0][:, 1:NE], beyond[:, 0:NE - 1]))
            shift, n = 1, 0
            while shift < NE:
                src, dst = first[n % 2], first[(n + 1) % 2]
                step(dve.tensor_copy(dst[:, 0:shift], src[:, 0:shift]))
                tt(dst[:, shift:NE], src[:, shift:NE], src[:, 0:NE - shift], ALU.add)
                shift, n = 2 * shift, n + 1
            first, other = first[n % 2], first[(n + 1) % 2]
            ts(first, first, float(MAIN), ALU.add)
            ts(other, first, -float(TILE), ALU.add)
            tt(other, other, ebase, ALU.subtract)
            ts(rank_mul, ranks, float(TILE), ALU.is_ge)
            tt(rank_mul, rank_mul, other.unsqueeze(1).to_broadcast(full), ALU.mult)
            tt(ranks, ranks, ebase.unsqueeze(1).to_broadcast(full), ALU.add)
            tt(ranks, ranks, rank_mul, ALU.add)
            for k in range(2):
                tt(rank_mul, ranks, onehot[k], ALU.mult)
                step(dve.tensor_reduce(rows_f[:, :, k], rank_mul, X, ALU.add))
            dve.tensor_copy(rows_i, rows_f).then_inc(rows_ready, 1)
            for j in range(EXTRA):
                ts(tab_f[0:1, 0, j], counts[0:1], float(TILE * (j + 1)), ALU.is_gt)
                ts(tab_f[0:1, 1, j], first[0:1], float(TILE * j), ALU.add)
                ts(tab_f[0:1, 1, j], tab_f[0:1, 1, j], float(NROWS - TILE), ALU.min)
            step(dve.tensor_copy(table[:, 0:2 * NE * EXTRA].rearrange("p (a e j) -> p a j e", a=2, j=EXTRA),
                                 tab_f[0:1]))
            step(dve.tensor_reduce(s_a[0:1, 0:1], counts[0:1], X, ALU.max))
            ts(s_a[0:1, 0:1], s_a[0:1, 0:1], float(TILE), ALU.is_gt)
            dve.tensor_copy(table[:, 2 * NE * EXTRA:2 * NE * EXTRA + 1], s_a[0:1, 0:1]).then_inc(counts_ready, 1)
            dve.wait_ge(counts_ready, 1)

            def hidden(e, par):
                dve.wait_ge(silu_ready, e + 1)
                dve.tensor_tensor(h[par], ps[0:TILE, 3, :], silu[par], ALU.mult).then_inc(h_ready, 1)
                dve.wait_ge(ht_done, e + 1)
                dve.tensor_copy(h_t[par], ps[:, 4, 0:4 * TILE]).then_inc(hT_ready, 1)

            def result(e, par, i, first):
                dve.wait_ge(dn_done, e + 1)
                if not first:
                    dve.wait_ge(y_stored[par], i * 16)
                dve.tensor_copy(y_sb[par].rearrange("p (h n) -> p h n", h=2), ps[0:TILE, 6:8, :]).then_inc(y_ready, 1)

            for e in range(2):
                hidden(e, e)
                result(e, e, 0, True)
            with dve.Fori(1, NE // 2) as i:
                for par in range(2):
                    hidden(2 * i + par, par)
                    result(2 * i + par, par, i, False)

            def more(i, row, m):
                dve.wait_ge(ov_act, m * 2)
                dve.tensor_tensor(h[0], ps[0:TILE, 3, :], silu[0], ALU.mult).then_inc(ov_dve, 1)
                dve.wait_ge(ov_pe, m * 4 - 1)
                dve.tensor_copy(h_t[0], ps[:, 4, 0:4 * TILE]).then_inc(ov_dve, 1)
                dve.wait_ge(ov_pe, m * 4)
                dve.tensor_copy(y_sb[0].rearrange("p (h n) -> p h n", h=2), ps[0:TILE, 6:8, :]).then_inc(ov_dve, 1)

            overflow(dve, more)
            dve.wait_ge(g_in, 48)
            for i in range(TT):
                r = ROWS[i]
                dve.wait_ge(gathered[i], 32)
                xi = x_tok[:r, i, :]
                stt(xi, at(2 * i * D, D, r), weight[:r, i, 0:1], xi, ALU.mult, ALU.add)
                dve.scalar_tensor_tensor(out=xi, in0=at((2 * i + 1) * D, D, r), scalar=weight[:r, i, 1:2], in1=xi,
                                         op0=ALU.mult, op1=ALU.add).then_inc(sum_ready, 1)
                dve.wait_ge(sum_ready, i + 1)
                dve.wait_ge(squares3, i + 1)
                mean, root_i = ss[:r, i:i + 1], rstd[:r, i:i + 1]
                dve.tensor_scalar(mean, mean, 1.0 / D, EPS, ALU.mult, ALU.add).then_inc(mean3, 1)
                dve.wait_ge(mean3, i + 1)
                dve.wait_ge(root3, i + 1)
                inverse_root(mean, root_i)
                dve.scalar_tensor_tensor(out=xn2[:r, i, :], in0=xi, scalar=root_i, in1=g_b[:r],
                                         op0=ALU.mult, op1=ALU.mult).then_inc(final_ready, 1)

        @block.tensor
        def _(pe):
            def begin(name):
                i = NUM[name]
                if i >= 4:
                    owner = TASKS[i - 4][1]
                    pe.wait_ge(emptied[owner], emptied_by(owner, i - 4))
                return pair(i)

            def end(ins):
                ins.then_inc(psum_ready, 1)

            pe.wait_ge(consts, 1)
            pe.wait_ge(small_in, 16 * 8)
            pe.wait_ge(dt_ready, 2)
            pe.wait_ge(c_loaded, 16 * 8)
            dst = begin("par")
            pe.transpose(dst[:, 0, 0:92], par_rows, ident[0:92, 0:92])
            for g in range(4):
                pe.transpose(dst[:, 0, 128 + 15 * g:143 + 15 * g], cache_rows[:, g * P:(g + 1) * P],
                             ident[0:HIST, 0:HIST])
            for n in range(4):
                last = pe.transpose(dst[:, 1, n * P:(n + 1) * P], c_in[:, n * P:(n + 1) * P], ident)
            end(last)
            for i in range(TT):
                dst, r = begin(f"xt{i}"), ROWS[i]
                pe.wait_ge(xn_ready, i + 1)
                for k in range(KD):
                    last = pe.transpose(dst[:, k // 4, (k % 4) * P:(k % 4) * P + r],
                                        xn_row[i % 2][:r, k * P:(k + 1) * P], ident[0:r, 0:r])
                end(last)
            pe.wait_ge(emptied["act"], emptied_by("act", NUM["xt4"]))

            def project(name, w, rhs, m, kk):
                dst = begin(name)
                for hh in range(2):
                    for k in range(kk):
                        last = pe.matmul(dst[:, hh, 0:HALF], w[:, k, m * P:(m + 1) * P],
                                         rhs[:, k, hh * HALF:(hh + 1) * HALF], start=(k == 0), stop=(k == kk - 1))
                end(last)

            def arrived(b):
                pe.wait_ge(w_stream[b % 2], 16 * (b // 2 + 1))
                return w_slot(b % 2, 4 if b in (6, 7) else 8)

            w = arrived(0)
            for m in range(4):
                project(f"u{m}", w, xn_t, m, KD)
            w = arrived(1)
            for m in range(4):
                project(f"gs{m}", w, xn_t, m, KD)
            dst = begin("kt")
            pe.wait_ge(bbd_ready, 4)
            pe.wait_ge(cpow_ready, 1)
            for j in range(NJ):
                for r in range(2):
                    last = pe.matmul(dst[32 * (j % 4):32 * (j % 4) + 32, 0, (j // 4) * P:(j // 4 + 1) * P],
                                     bbd[:, (2 * j + r) * 32:(2 * j + r + 1) * 32], cpow[r][:, j * 144:j * 144 + P],
                                     start=(r == 0), stop=(r == 1))
            end(last)
            pe.wait_ge(s_ready, 1)
            for r in range(4):
                dst = begin(f"st{r}")
                for n in range(8):
                    last = pe.transpose(dst[:, n // 4, (n % 4) * P:(n % 4 + 1) * P],
                                        s_nat[:, (8 * r + n) * P:(8 * r + n + 1) * P], ident)
                end(last)
            pe.wait_ge(emptied["act"], emptied_by("act", NUM["u3"]))
            for r in range(4):
                dst = begin(f"uc{r}")
                for hh in range(2):
                    for b in range(4):
                        frames = u_t[:, b, :].rearrange("p (c s) -> p s c", s=L)[:, 2 * r + hh, :]
                        last = pe.transpose(dst[0:NC, hh, b * P:(b + 1) * P], frames, ident)
                end(last)
            pe.wait_ge(emptied["dve"], emptied_by("dve", NUM["uc3"]))
            for r in range(4):
                dst = begin(f"usq{r}")
                for n in range(8):
                    last = pe.transpose(dst[:, n // 4, (n % 4) * NC:(n % 4 + 1) * NC], uc[0:NC, (8 * r + n) * P:(8 * r + n + 1) * P],
                                        ident[0:NC, 0:NC])
                end(last)
            pe.wait_ge(emptied["act"], emptied_by("act", NUM["usq3"]))
            for r in range(3):
                dst = begin(f"v{r}")
                for n in range(min(6, NJ - 6 * r)):
                    j = 6 * r + n
                    for ri in range(2):
                        for g in range(2):
                            o = (2 * (n % 3) + ri) * NC
                            last = pe.matmul(dst[64 * g:64 * g + 64, n // 3, o:o + NC],
                                             s_t[:, (2 * j + ri) * P + 64 * g:(2 * j + ri) * P + 64 * g + 64],
                                             usq[:, (2 * j + g) * NC:(2 * j + g + 1) * NC], start=True, stop=True)
                end(last)
            w = arrived(2)
            for m in range(4):
                project(f"gs{m + 4}", w, xn_t, m, KD)
            pe.wait_ge(toep_in, 16 * L * 4)
            pe.wait_ge(hpad_ready, 6)
            for r in range(4):
                dst = begin(f"y{r}")
                for n in range(8):
                    g = 8 * r + n
                    j, o = g // 2, dst[0:NC, n // 4, (n % 4) * P:(n % 4 + 1) * P]
                    pe.matmul(o, usq[:, g * NC:(g + 1) * NC], toep[:, g * P:(g + 1) * P], start=True, stop=False)
                    for ri in range(2):
                        last = pe.matmul(o, hpad[:, j, ri, g % 2, :], cpow[ri][:, j * 144 + Q:j * 144 + Q + P],
                                         start=False, stop=(ri == 1))
                end(last)
            for b in range(4):
                dst = begin(f"gt{b}")
                if b == 0:
                    pe.wait_ge(emptied["act"], emptied_by("act", NUM["y3"]))
                for t in range(L):
                    last = pe.transpose(dst[:, t // 4, (t % 4) * NC:(t % 4 + 1) * NC],
                                        gc[0:NC, t * 512 + b * P:t * 512 + (b + 1) * P], ident[0:NC, 0:NC])
                end(last)
            dst = begin("fin")
            pe.wait_ge(fin_ready, 2)
            end(pe.transpose(dst[0:64, 0, 0:P], fin_cols, ident))
            w = arrived(3)
            for m in range(4):
                project(f"up{m}", w, xn_t, m, KD)
            dst = begin("hist")
            pe.wait_ge(emptied["act"], emptied_by("act", NUM["up3"]))
            for n, c in enumerate((SEQ, UPW - HIST)):
                for g in range(4):
                    last = pe.transpose(dst[0:HIST, n, g * P:(g + 1) * P], up_t[:, g, c:c + HIST], ident)
            end(last)
            for b in (4, 5):
                w = arrived(b)
                for m in range(4):
                    project(f"gp{m + 4 * (b - 4)}", w, xn_t, m, KD)
            w_a, w_b = arrived(6), arrived(7)
            pe.wait_ge(emptied["dve"], emptied_by("dve", NUM["gt3"]))
            pe.wait_ge(pw_in, 16)
            pe.wait_ge(z_ready, 4)
            for m in range(8):
                project(f"gb{m}", w_b, g_t, m, 4)
                project(f"ga{m}", w_a, g_t, m, 4)
                dst, g = begin(f"po{m}"), m // 2
                for hh in range(2):
                    last = pe.matmul(dst[:, hh, 0:HALF], pool_w[:, g * 256 + (m % 2) * P:g * 256 + (m % 2) * P + P],
                                     z_t[:, g, hh * HALF:(hh + 1) * HALF], start=True, stop=True)
                end(last)
            w0, w1 = arrived(8), arrived(9)
            pe.wait_ge(merged, 8)

            def out_proj(i):
                dst, r = begin(f"out{i}"), ROWS[i]
                for n, wn in enumerate((w0, w1)):
                    for k in range(8):
                        last = pe.matmul(dst[:r, n, :], m_t[:, k, i * P:i * P + r], wn[:, k, :],
                                         start=(k == 0), stop=(k == 7))
                end(last)

            out_proj(0)
            for i in range(TT):
                if i + 1 < TT:
                    out_proj(i + 1)
                dst, r = begin(f"x2t{i}"), ROWS[i]
                pe.wait_ge(xn2_ready, i + 1)
                for k in range(KD):
                    last = pe.transpose(dst[:, k // 4, (k % 4) * P:(k % 4) * P + r],
                                        xn2[:r, i, k * P:(k + 1) * P], ident[0:r, 0:r])
                end(last)
            dst = begin("lg")
            pe.wait_ge(emptied["act"], emptied_by("act", NUM["x2t4"]))
            pe.wait_ge(wr_in, 32)
            for i in range(TT):
                for k in range(KD):
                    last = pe.matmul(dst[:ROWS[i], 0, i * 36:(i + 1) * 36], xn2_t[:, k, i * P:i * P + ROWS[i]],
                                     w_r[:, k, :], start=(k == 0), stop=(k == KD - 1))
            end(last)
            dst = begin("rank")
            pe.wait_ge(chosen_ready, 1)
            pe.wait_ge(consts, 2)
            for i in range(TT):
                r = ROWS[i]
                o = dst[:r, 0, i * NE:(i + 1) * NE]
                for n in range(i):
                    pe.matmul(o, ones[:, :r], chosen[:, n, :], start=(n == 0), stop=False)
                pe.matmul(o, tri[:r, :r], chosen[:r, i, :], start=(i == 0), stop=True)
            for i in range(TT):
                last = pe.matmul(dst[:, 1, 0:NE], ones[:ROWS[i], :], chosen[:ROWS[i], i, :],
                                 start=(i == 0), stop=(i == TT - 1))
            end(last)

            def turn(x, s):
                for k in range(KD):
                    turned = (ps[:, k // 4, (k % 4) * TILE:(k % 4 + 1) * TILE], x[:, k * P:(k + 1) * P],
                              ident[0:TILE, 0:TILE])
                    last = pe.transpose(*turned) if k else pe.matmul(*turned, start=True, stop=True)
                last.then_inc(s, 1)

            def gate_up(x_t, par, s):
                for n, sl in enumerate((GATE[par], UP[par])):
                    wn = w_slot(sl, 8)
                    for k in range(KD):
                        last = pe.matmul(ps[0:TILE, 2 + n, :], x_t[:, k * TILE:(k + 1) * TILE], wn[:, k, :],
                                         start=(k == 0), stop=(k == KD - 1))
                last.then_inc(s, 1)

            def turn_h(hh, s):
                for k in range(4):
                    turned = ps[:, 4, k * TILE:(k + 1) * TILE], hh[:, k * P:(k + 1) * P], ident[0:TILE, 0:TILE]
                    last = pe.transpose(*turned) if k else pe.matmul(*turned, start=True, stop=True)
                last.then_inc(s, 1)

            def down(hh_t, par, s):
                wn = w_slot(DOWN[par], 4)
                for n in range(2):
                    for k in range(4):
                        last = pe.matmul(ps[0:TILE, 6 + n, :], hh_t[:, k * TILE:(k + 1) * TILE],
                                         wn[:, k, n * 512:(n + 1) * 512], start=(k == 0), stop=(k == 3))
                last.then_inc(s, 1)

            def expert(e, i, par, first=False, final=False):
                pe.wait_ge(xgt_ready, e + 1)
                pe.wait_ge(wg_in[par], i * 16 + 16)
                pe.wait_ge(wu_in[par], i * 16 + 16)
                gate_up(xg_t[par], par, gu_done)
                if not final:
                    pe.wait_ge(xg_in[1 - par], (i + par) * 16 + 16)
                    turn(xg[1 - par], xt_done)
                pe.wait_ge(h_ready, e + 1)
                turn_h(h[par], ht_done)
                pe.wait_ge(hT_ready, e + 1)
                pe.wait_ge(wd_in[par], i * 16 + 16)
                if not first:
                    pe.wait_ge(y_ready, e)
                down(h_t[par], par, dn_done)

            pe.wait_ge(emptied["dve"], emptied_by("dve", NUM["rank"]))
            pe.wait_ge(xg_in[0], 16)
            turn(xg[0], xt_done)
            expert(0, 0, 0, first=True)
            expert(1, 0, 1)
            with pe.Fori(1, NE // 2 - 1) as i:
                for par in range(2):
                    expert(2 * i + par, i, par)
            expert(NE - 2, NE // 2 - 1, 0)
            expert(NE - 1, NE // 2 - 1, 1, final=True)
            pe.wait_ge(counts_ready, 1)

            def more(i, row, n):
                pe.wait_ge(ov_x, n * 16)
                turn(xg[0], ov_pe)
                pe.wait_ge(ov_act, n * 2 - 1)
                pe.wait_ge(ov_w, n * 48)
                gate_up(xg_t[0], 0, ov_pe)
                pe.wait_ge(ov_dve, n * 3 - 2)
                turn_h(h[0], ov_pe)
                pe.wait_ge(ov_dve, n * 3 - 1)
                down(h_t[0], 0, ov_pe)

            overflow(pe, more)


_INS = ["x_prompt", "x_sample", "state_ssm_re", "state_ssm_im", "cache_pool", "g_mix", "w_in", "ssm_a_re",
        "ssm_a_im", "ssm_log_dt", "ssm_b_re", "ssm_b_im", "ssm_c_re", "ssm_c_im", "ssm_d", "w_glu_a", "w_glu_b",
        "pool_w", "pool_scale", "w_out", "g_ffn", "w_router_group", "w_router_expert", "w_exp_gate", "w_exp_up",
        "w_exp_down", "g_final"]
_OUTS = [("y_prompt", (1, SEQ, D)), ("y_sample", (1, DEC, D)), ("re_p", (1, 1, G, N)), ("im_p", (1, 1, G, N)),
         ("hist_p", (1, 1, HIST, 512)), ("re_s", (1, 1, G, N)), ("im_s", (1, 1, G, N)), ("hist_s", (1, 1, HIST, 512))]


def kernel(**inputs):
    import numpy as _np
    import concourse.bacc as _bacc
    from concourse import mybir as _mybir
    from concourse.bass_utils import run_bass_kernel_spmd as _run

    nc = _bacc.Bacc("TRN2", target_bir_lowering=False, num_devices=1)
    arrays, args, outs = {}, {}, {}
    for name in _INS:
        arr = _np.ascontiguousarray(inputs[name])
        arrays[f"in_{name}"] = arr
        args[name] = nc.dram_tensor(f"in_{name}", arr.shape, _mybir.dt.from_np(arr.dtype), kind="ExternalInput").ap()
    for name, shape in _OUTS:
        outs[name] = nc.dram_tensor(f"out_{name}", shape, F32, kind="ExternalOutput").ap()
    encoder_step(nc, args, outs)
    r = _run(nc, [arrays], core_ids=[0])
    return tuple(r.results[0][f"out_{name}"] for name, _ in _OUTS)
```

```python
from contextlib import ExitStack

import concourse.bass as bass
from concourse import mybir

ALU = mybir.AluOpType
ACT = mybir.ActivationFunctionType
F32 = mybir.dt.float32
I32 = mybir.dt.int32
F32R = mybir.dt.float32r
X = mybir.AxisListType.X

P = 128
D = 1024
SEQ, DEC = 512, 32
NT = SEQ + DEC
TT = 5
ROWS = [128, 128, 128, 128, 32]
KD = D // P
L = 8
NC = NT // L
PC = SEQ // L
G, N, Q = 32, 64, 16
NJ = G // 2
HIST = 15
WINDOWS = (2, 4, 8, 16)
NE, EG, EI = 32, 4, 8
F = 512
TILE = 64
EXTRA = (NT + TILE - 1) // TILE - 1
EPS = 1e-6
BIG = 3.0e38
MAIN = NE * TILE
NROWS = -(-(MAIN + 2 * NT + TILE) // P) * P
ZEROED = NROWS // P + (NROWS - MAIN) // P
HALF = NT // 2

SLOT = 4096
O_TOEP = 2 * SLOT
O_SGP = O_TOEP
O_GT = O_SGP + 8 * NT
O_POOLW = O_GT + 4 * NT
O_XTOK = 4 * SLOT
O_GB = O_XTOK + TT * D
O_MISC = O_GB + D
O_CPOW = O_MISC + 1728
O_UPT = O_CPOW
UPW = HIST + SEQ + HIST + DEC
O_Z = O_UPT + 4 * UPW
O_UT = O_CPOW + 2 * NJ * 9 * Q
O_USQ = O_UT + 4 * NT
O_V = O_USQ + G * NC
O_WR = O_V + NJ * 2 * NC
END = O_WR + 8 * 36
O_XN2 = O_CPOW
O_JUNK = O_XN2 + TT * D
O_ROUT = O_JUNK + D
O_ST = 3 * SLOT
O_SNAT = END
O_UC = O_SNAT + SLOT
O_GC = O_SNAT
O_HPAD = O_UC
O_XNT = O_HPAD + NJ * 4 * NC
O_MT = O_XNT
O_SGS = O_XNT + KD * NT
O_XN2T = O_SGS
FRONT_END = O_SGS + KD * NT
M_ID, M_PAR, M_HIST, M_PW, M_A4, M_TMP, M_SS, M_FIN, M_TRI, M_INV, M_MASK, M_EB = (
    0, 128, 228, 288, 576, 640, 1120, 1152, 1280, 1408, 1472, 1504)
M_ONES = 1600

TASKS = [("par", "dve")] + [(f"xt{i}", "act") for i in range(TT)]
TASKS += [(f"u{m}", "act") for m in range(4)] + [(f"gs{m}", "act") for m in range(4)]
TASKS += [("kt", "dve")] + [(f"st{r}", "act") for r in range(4)]
TASKS += [(f"uc{r}", "dve") for r in range(4)] + [(f"usq{r}", "act") for r in range(4)]
TASKS += [(f"v{r}", "dve") for r in range(3)] + [(f"gs{m}", "act") for m in range(4, 8)]
TASKS += [(f"y{r}", "act") for r in range(4)] + [(f"gt{b}", "dve") for b in range(4)]
TASKS += [("fin", "dve")] + [(f"up{m}", "act") for m in range(4)] + [("hist", "act")]
TASKS += [(f"gp{m}", "act") for m in range(8)]
for _m in range(8):
    TASKS += [(f"gb{_m}", "act"), (f"ga{_m}", "dve"), (f"po{_m}", "dve")]
TASKS += [("out0", "dve"), ("out1", "dve"), ("x2t0", "act"), ("out2", "dve"), ("x2t1", "act"),
          ("out3", "dve"), ("x2t2", "act"), ("out4", "dve"), ("x2t3", "act"), ("x2t4", "act"),
          ("lg", "dve"), ("rank", "dve")]
NUM = {name: i for i, (name, _) in enumerate(TASKS)}


def emptied_by(owner, i):
    return sum(1 for _, o in TASKS[:i + 1] if o == owner)


def encoder_step(nc, a, out):
    ctx = ExitStack()
    with ctx:
        arena = ctx.enter_context(nc.sbuf_tensor("arena", [P, END], F32))
        with nc.sbuf_tensor("front", [P, FRONT_END - END], F32) as front:
            pass
        split = ctx.enter_context(nc.sbuf_tensor("split", [P, FRONT_END - END], F32R))
        ps = ctx.enter_context(nc.psum_tensor("ps", [P, 8, 512], F32))
        x_rows = nc.dram_tensor("x_rows", (NROWS, D), F32).ap()
        y_rows = nc.dram_tensor("y_rows", (NROWS, D), F32).ap()
        kd = nc.dram_tensor("k_taps", (P, 512), F32).ap()

        def sem(name):
            return ctx.enter_context(nc.semaphore(name))

        def at(offset, words, rows=P, row0=0):
            if offset >= END:
                return front[row0:row0 + rows, offset - END:offset - END + words]
            return arena[row0:row0 + rows, offset:offset + words]

        def misc(offset, words, rows=P, row0=0):
            return at(O_MISC + offset, words, rows, row0)

        def slot(s):
            return at(s * SLOT, SLOT)

        def pair(i):
            return ps[:, 2 * (i % 4):2 * (i % 4) + 2, :]

        ident, tri = misc(M_ID, 128), misc(M_TRI, 128)
        prm = misc(M_PAR, 92)
        hist_t = misc(M_HIST, 60).rearrange("p (g c) -> p g c", g=4)
        powers = misc(M_PW, 288).rearrange("p (r t j) -> p r t j", r=2, t=9)
        a4 = misc(M_A4, 64).rearrange("p (j o i) -> p j o i", j=NJ, o=2)
        ss, rstd = misc(M_SS, TT), misc(M_SS + 8, TT)
        fin_cols = misc(M_FIN, 64)
        inv = misc(M_INV, 60).rearrange("p (g c) -> p g c", g=4)
        diag16 = misc(M_MASK, 16)
        ebase = misc(M_EB, 32)
        ones = misc(M_ONES, P)
        x_tok = at(O_XTOK, TT * D).rearrange("p (i d) -> p i d", i=TT)
        g_b = at(O_GB, D)
        xn_t = at(O_XNT, KD * NT).rearrange("p (k t) -> p k t", k=KD)
        sgs = at(O_SGS, 8 * NT).rearrange("p (m t) -> p m t", m=8)
        sgp = at(O_SGP, 8 * NT).rearrange("p (m t) -> p m t", m=8)
        m_t = at(O_MT, 8 * NT).rearrange("p (m t) -> p m t", m=8)
        u_t = at(O_UT, 4 * NT).rearrange("p (m t) -> p m t", m=4)
        up_t = at(O_UPT, 4 * UPW).rearrange("p (g c) -> p g c", g=4)
        z_t = at(O_Z, 4 * NT).rearrange("p (g t) -> p g t", g=4)
        cpow = [at(O_CPOW + r * NJ * 144, NJ * 144) for r in range(2)]
        usq, v_all = at(O_USQ, G * NC), at(O_V, NJ * 2 * NC)
        v = v_all.rearrange("p (j r c) -> p j r c", j=NJ, r=2)
        s_nat, s_t = at(O_SNAT, 32 * P), at(O_ST, 32 * P)
        toep = at(O_TOEP, G * P)
        uc = at(O_UC, L * 512)
        gc = at(O_GC, L * 512)
        hpad = at(O_HPAD, NJ * 4 * NC).rearrange("p (j r g c) -> p j r g c", j=NJ, r=2, g=2)
        g_t = at(O_GT, 4 * NT).rearrange("p (b t) -> p b t", b=4)
        pool_w = at(O_POOLW, D)
        par_rows = at(O_UT, 128, 92)
        dt_rows = at(O_UT + 128, 2, NJ, 64)
        c_in = at(O_USQ, 512)
        c_t = at(O_USQ + 512, 512).rearrange("p (r j q) -> p r j q", r=2, j=NJ)
        bbd = at(O_USQ + 1024, 1024)
        b_in = at(O_V, 512).rearrange("p (r j q) -> p r j q", r=2, j=NJ)
        bbar = at(O_V + 512, 512).rearrange("p (r j q) -> p r j q", r=2, j=NJ)
        k_sb = at(O_V + 1024, 512)
        cache_rows = at(O_UT + 256, 512, HIST)
        prod = at(O_ST, NJ * 144)
        zeros = at(O_UC, D)
        xn_row = [at(O_UC + D, D), at(O_UC + 2 * D, D)]
        junk0 = at(O_UC + 3 * D, D)
        scan_tmp = at(O_UT, 64).rearrange("p (j o i) -> p j o i", j=NJ, o=2)
        scan_red = at(O_UT + 64, 32).rearrange("p (j o) -> p j o", j=NJ)
        sig_b = [at(O_UT + n * NT, NT) for n in range(2)]
        t1 = [at(O_UT + (2 + n) * NT, NT) for n in range(2)]
        t2 = [at(O_UT + (4 + n) * NT, NT) for n in range(2)]
        win = [at(O_UT + 6 * NT + n * UPW, UPW) for n in range(2)]
        fin_rows = at(O_UT + 8 * NT + 64, 128, 64)
        hist_rows = at(O_UT + 8 * NT + 256, 2 * 512, HIST)
        w_r = at(O_WR, 8 * 36).rearrange("p (k n) -> p k n", k=KD)
        xn2 = at(O_XN2, TT * D).rearrange("p (i d) -> p i d", i=TT)
        xn2_t = at(O_XN2T, KD * NT).rearrange("p (k t) -> p k t", k=KD)
        junk1 = at(O_JUNK, D)
        PAIR = 2 * TILE
        CHUNK = SLOT // 2
        w_hi, w_lo = ([split[:, (3 * n + i) * CHUNK:(3 * n + i + 1) * CHUNK] for i in range(3)] for n in range(2))
        x_split = [split[:, 6 * CHUNK + n * KD * PAIR:6 * CHUNK + (n + 1) * KD * PAIR] for n in range(2)]
        h_split = split[:, 6 * CHUNK + 2 * KD * PAIR:6 * CHUNK + (2 * KD + 4) * PAIR]
        xg = [at(O_XN2 + n * D, D, TILE) for n in range(2)]
        gu_rows = at(O_XN2 + 2 * D, 2 * F, PAIR)
        y_lo = at(O_XN2 + 3 * D, D, TILE)
        y_sb = at(O_XN2 + 4 * D, D, TILE)
        silu = at(O_JUNK, 4 * TILE)
        h = at(O_JUNK + 4 * TILE, 4 * TILE)
        fold = misc(M_TMP, TILE)
        GATE, UP, DOWN = 2, 3, 0

        place = [O_ROUT]

        def small(*shape):
            words = 1
            for s in shape:
                words *= s
            ap = at(place[0], words)
            place[0] += words
            assert place[0] <= END
            if len(shape) == 2:
                return ap.rearrange("p (a b) -> p a b", a=shape[0])
            if len(shape) == 3:
                return ap.rearrange("p (a b c) -> p a b c", a=shape[0], b=shape[1])
            if len(shape) == 4:
                return ap.rearrange("p (a b c d) -> p a b c d", a=shape[0], b=shape[1], c=shape[2])
            return ap

        logits = small(TT, 36)
        onehot = [small(TT, NE) for _ in range(2)]
        chosen = small(TT, NE)
        weight = small(TT, 2)
        rows_f = small(TT, 2)
        rows_i = small(TT, 2).bitcast(I32)
        ranks = small(TT, NE)
        s_a, s_b, s_c, s_d = (small(TT) for _ in range(4))
        g_hot, g_exp = small(TT, EG), small(TT, EG)
        le_sel, i_hot = small(TT, EI), [small(TT, EI) for _ in range(2)]
        i_tmp = small(TT, EI)
        le_mul = small(TT, EG, EI)
        prefer = small(EI)
        counts = small(NE)
        tab_f = small(2, EXTRA, NE)
        rank_mul = small(TT, NE)
        e_neg = small(TT)
        table = small(2 * NE * EXTRA + 8)[0:1].bitcast(I32)

        x_in, small_in, b_loaded, c_loaded = sem("x_in"), sem("small_in"), sem("b_loaded"), sem("c_loaded")
        dt_ready = sem("dt_ready")
        g_in, w_stream, pw_in, wr_in = sem("g_in"), [sem("w_stream0"), sem("w_stream1")], sem("pool_w_in"), sem("router_w_in")
        consts, zero_ready, rows_zeroed = sem("consts"), sem("zero_ready"), sem("rows_zeroed")
        toep_zero, taps_ready, taps_out, toep_in = sem("toep_zero"), sem("taps_ready"), sem("taps_out"), sem("toep_in")
        psum_ready = sem("psum_ready")
        emptied = {"act": sem("emptied_act"), "dve": sem("emptied_dve")}
        squares, mean_sq, root, xn_ready = sem("squares"), sem("mean_sq"), sem("root"), sem("xn_ready")
        step_dve, step_pool, ss_ready = sem("step_dve"), sem("step_pool"), sem("ss_ready")
        bbd_ready, cpow_ready, s_ready = sem("bbd_ready"), sem("cpow_ready"), sem("s_ready")
        hpad_zero, hpad_ready, scan_step, fin_ready = sem("hpad_zero"), sem("hpad_ready"), sem("scan_step"), sem("fin_ready")
        halo_ready, z_ready = sem("halo_ready"), sem("z_ready")
        gated, merged = sem("gated"), sem("merged")
        squares2, mean2, root2, xn2_ready = sem("squares2"), sem("mean2"), sem("root2"), sem("xn2_ready")
        neg_ready, exp_ready, chosen_ready, rows_ready = sem("neg_ready"), sem("exp_ready"), sem("chosen_ready"), sem("rows_ready")
        scattered, counts_ready = sem("scattered"), sem("counts_ready")
        outs_done = sem("outs_done")
        xg_in = [sem("xg_in0"), sem("xg_in1")]
        w_in = [sem(f"expert_{n}_in") for n in ("gate0", "gate1", "up0", "up1", "down0", "down1")]
        hi_ready, lo_ready, w_used = sem("w_hi_ready"), sem("w_lo_ready"), sem("w_used")
        xt_done, x_hi_ready, x_lo_ready = sem("xt_done"), sem("x_hi_ready"), sem("x_lo_ready")
        gu_ready, folded, silu_ready, h_ready = sem("gate_up_rows"), sem("folded"), sem("silu_ready"), sem("h_ready")
        h_hi_ready, h_lo_ready, y_lo_ready, y_ready = sem("h_hi_ready"), sem("h_lo_ready"), sem("y_lo_ready"), sem("y_ready")
        y_stored, y_free = sem("y_stored"), sem("y_free")
        ov_done = sem("overflow_done")
        gathered = [sem(f"gathered{i}") for i in range(TT)]
        sum_ready, squares3, mean3, root3, final_ready = sem("sum_ready"), sem("squares3"), sem("mean3"), sem("root3"), sem("final_ready")

        def psum_waits(eng, name):
            eng.wait_ge(psum_ready, NUM[name] + 1)

        experts = [a[f"w_exp_{n}"][0].rearrange("e (k p) n -> e p k n", p=P) for n in ("gate", "up", "down")]

        def w_slot(s, k):
            return slot(s).rearrange("p (k n) -> p k n", k=k)

        def chunk(c):
            return at((GATE, UP, DOWN)[c // 2] * SLOT + (c % 2) * CHUNK, CHUNK)

        def chunk_source(e, c):
            n = 4 if c < 4 else 2
            src = experts[c // 2][bass.ds(e, 1)].rearrange("o p k n -> (o p) k n")
            return src[:, n * (c % 2):n * (c % 2) + n, :]

        def load_chunk(sp, e, c):
            dst = chunk(c).rearrange("p (k n) -> p k n", k=4 if c < 4 else 2)
            sp.dma_start(dst, chunk_source(e, c)).then_inc(w_in[c], 16)

        def number(e, c, first=False):
            return c if first else 6 * e + (c - 2)

        def parts_of(c, first=False):
            i = c % 3 if first else (c + 1) % 3
            return w_hi[i], w_lo[i]

        def overflow(eng, body):
            any_extra = eng.value_load(table[0:1, 2 * NE * EXTRA:2 * NE * EXTRA + 1], min_val=0, max_val=1)
            count = eng.alloc_register()
            eng.reg_mov(count, 1)
            with eng.If(any_extra > 0):
                with eng.Fori(0, NE * EXTRA) as i:
                    used = eng.value_load(table[0:1, bass.ds(i, 1)], min_val=0, max_val=1)
                    with eng.If(used > 0):
                        e_row = eng.value_load(table[0:1, bass.ds(i + NE * EXTRA, 1)],
                                               min_val=0, max_val=NROWS - TILE)
                        body(i, e_row, eng.snap(count, min_val=1, max_val=NE * EXTRA + 1))
                        eng.reg_add(count, count, 1)

        block = ctx.enter_context(nc.Block())

        @block.sync
        def _(sp):
            for i in range(TT):
                src = a["x_prompt"][0, i * P:(i + 1) * P] if i < 4 else a["x_sample"][0]
                sp.dma_start(x_tok[:ROWS[i], i, :], src).then_inc(x_in, 16)
            w_in = a["w_in"][0].rearrange("(k p) (b n) -> b p k n", p=P, b=6)
            glu = [a[n][0].rearrange("(k p) n -> p k n", p=P) for n in ("w_glu_a", "w_glu_b")]
            w_out = a["w_out"][0].rearrange("(k p) (b n) -> b p k n", p=P, b=2)
            stream = [(w_in[0], 8, "u3"), (w_in[2], 8, "gs3"), (w_in[3], 8, "gs7"), (w_in[1], 8, "up3"),
                      (w_in[4], 8, "gp3"), (w_in[5], 8, "gp7"), (glu[0], 4, "ga7"), (glu[1], 4, "gb7"),
                      (w_out[0], 8, None), (w_out[1], 8, None)]
            for b, (src, k, _) in enumerate(stream):
                if b >= 2:
                    psum_waits(sp, stream[b - 2][2])
                if b == 7:
                    sp.dma_start(pool_w.rearrange("p (g n) -> p g n", g=4),
                                 a["pool_w"][0].rearrange("g p n -> p g n")).then_inc(pw_in, 16)
                sp.dma_start(w_slot(b % 2, k), src).then_inc(w_stream[b % 2], 16)
                if b == 5:
                    sp.wait_ge(emptied["dve"], emptied_by("dve", NUM["fin"]))
                    for n, name in enumerate(("re_p", "im_p", "re_s", "im_s")):
                        sp.dma_start(out[name].rearrange("a b (j g) n -> (a b j) (g n)", g=2),
                                     fin_rows[16 * n:16 * n + 16, :]).then_inc(outs_done, 16)
            sp.wait_ge(emptied["act"], emptied_by("act", NUM["hist"]))
            for n, name in enumerate(("hist_p", "hist_s")):
                sp.dma_start(out[name][0, 0], hist_rows[:, n * 512:n * 512 + 512]).then_inc(outs_done, 16)

            def load(e, par):
                sp.wait_ge(xt_done, e - 1)
                sp.dma_start(xg[par], x_rows[bass.ds(e * TILE, TILE), :]).then_inc(xg_in[par], 16)
                for c in range(6):
                    sp.wait_ge(lo_ready, number(e - 1, c + 1))
                    load_chunk(sp, e if c < 4 else e - 1, c)

            sp.wait_ge(merged, 8)
            psum_waits(sp, "po7")
            sp.wait_ge(emptied["dve"], emptied_by("dve", NUM["po7"]))
            for c in range(4):
                load_chunk(sp, 0, c)
            psum_waits(sp, "out4")
            for c in (4, 5):
                load_chunk(sp, 0, c)
            sp.wait_ge(scattered, 16 * 2 * TT)
            for e in range(2):
                sp.dma_start(xg[e], x_rows[e * TILE:(e + 1) * TILE, :]).then_inc(xg_in[e], 16)
            for c in range(4):
                sp.wait_ge(lo_ready, c + 1)
                load_chunk(sp, 1, c)
            with sp.Fori(1, NE // 2) as i:
                for par in range(2):
                    load(2 * i + par, par)
            for c in (4, 5):
                sp.wait_ge(lo_ready, number(NE - 1, c + 1))
                load_chunk(sp, NE - 1, c)

            sp.wait_ge(counts_ready, 1)

            def more(i, row, n):
                sp.wait_ge(ov_done, n)
                sp.dma_start(xg[0], x_rows[bass.ds(row, TILE), :]).then_inc(xg_in[0], 16)
                for c in range(6):
                    load_chunk(sp, i // EXTRA, c)

            overflow(sp, more)
            for i in range(TT):
                sp.wait_ge(final_ready, i + 1)
                dst = out["y_prompt"][0, i * P:(i + 1) * P] if i < 4 else out["y_sample"][0]
                sp.dma_start(dst, xn2[:ROWS[i], i, :]).then_inc(outs_done, 16)
            sp.wait_ge(outs_done, 16 * (4 + 2 + TT))

        @block.gpsimd
        def _(pool):
            done = [0]

            def step(ins):
                done[0] += 1
                ins.then_inc(step_pool, 1)
                pool.wait_ge(step_pool, done[0])

            step(pool.memset(ident, 0.0))
            pool.affine_select(out=ident, in_=ident, compare_op=ALU.not_equal, fill=1.0, base=0,
                               pattern=[[-1, P]], channel_multiplier=1).then_inc(consts, 1)
            step(pool.memset(diag16, 0.0))
            for g in range(8):
                step(pool.affine_select(out=diag16, in_=diag16, compare_op=ALU.not_equal, fill=1.0, base=-16 * g,
                                        pattern=[[-1, 16]], channel_multiplier=1))
            step(pool.memset(tri, 1.0))
            pool.memset(ones, 1.0)
            step(pool.affine_select(out=tri, in_=tri, compare_op=ALU.is_gt, fill=0.0, base=0,
                                    pattern=[[1, P]], channel_multiplier=-1))
            for gi, w in enumerate(WINDOWS):
                for c in range(HIST):
                    pool.memset(inv[:, gi, c:c + 1], 1.0 / min(w, c + 1))
            pool.iota(ebase, pattern=[[TILE, NE]], base=0, channel_multiplier=0,
                      allow_small_or_imprecise_dtypes=True).then_inc(consts, 1)
            pool.memset(zeros, 0.0).then_inc(zero_ready, 1)
            pool.memset(bbd, 0.0).then_inc(toep_zero, 1)
            pool.memset(toep, 0.0).then_inc(toep_zero, 1)
            pool.wait_ge(zero_ready, 1)
            with pool.Fori(0, NROWS // P) as n:
                pool.dma_start(x_rows[bass.ds(n * P, P), :], zeros).then_inc(rows_zeroed, 16)
            with pool.Fori(MAIN // P, NROWS // P) as n:
                pool.dma_start(y_rows[bass.ds(n * P, P), :], zeros).then_inc(rows_zeroed, 16)
            pool.wait_ge(taps_ready, 4)
            pool.dma_start(kd, k_sb).then_inc(taps_out, 16)
            pool.wait_ge(taps_out, 16)
            pool.wait_ge(toep_zero, 2)
            taps = kd.rearrange("(g q) (b n) -> q b g n", q=Q, b=4)
            for s in range(L):
                dst = toep[16 * s:16 * s + 16].rearrange("q (b g n) -> q b g n", b=4, g=8)
                for b in range(4):
                    pool.dma_start(dst[:, b, :, 16 * s:P], taps[:, b, :, 0:P - 16 * s]).then_inc(toep_in, 16)
            psum_waits(pool, "usq3")
            pool.memset(at(O_HPAD, NJ * 4 * NC), 0.0).then_inc(hpad_zero, 1)
            psum_waits(pool, "y3")
            pool.memset(up_t[:, :, 0:HIST], 0.0).then_inc(halo_ready, 1)
            pool.tensor_copy(up_t[:, :, HIST + SEQ:2 * HIST + SEQ], hist_t).then_inc(halo_ready, 1)
            psum_waits(pool, "fin")
            for gi, w in enumerate(WINDOWS):
                pool.wait_ge(emptied["act"], emptied_by("act", NUM[f"up{gi}"]))
                pool.wait_ge(halo_ready, 2)
                src, span, n = up_t[:, gi, :], 1, 0
                while span < w:
                    dst = win[n % 2]
                    step(pool.tensor_tensor(dst[:, 2 * span - 1:UPW], src[:, 2 * span - 1:UPW],
                                            src[:, span - 1:UPW - span], ALU.add))
                    src, span, n = dst, 2 * span, n + 1
                z = z_t[:, gi, :]
                step(pool.tensor_scalar(z[:, 0:SEQ], src[:, HIST:HIST + SEQ], 1.0 / w, None, ALU.mult))
                step(pool.tensor_tensor(z[:, 0:HIST], src[:, HIST:2 * HIST], inv[:, gi, :], ALU.mult))
                step(pool.tensor_scalar(z[:, SEQ:NT], src[:, 2 * HIST + SEQ:UPW], 1.0 / w, None, ALU.mult))
                step(pool.tensor_tensor(z[:, 0:SEQ], z[:, 0:SEQ], up_t[:, gi, HIST:HIST + SEQ], ALU.subtract))
                pool.tensor_tensor(z[:, SEQ:NT], z[:, SEQ:NT], up_t[:, gi, 2 * HIST + SEQ:UPW],
                                   ALU.subtract).then_inc(z_ready, 1)
            pool.wait_ge(z_ready, 4)
            for n in range(PAIR // TILE):
                pool.wait_ge(consts, 2 + n)
                pool.tensor_copy(fold[n * TILE:(n + 1) * TILE],
                                 ident[n * TILE:(n + 1) * TILE, n * TILE:(n + 1) * TILE]).then_inc(consts, 1)
            pool.wait_ge(consts, 2 + PAIR // TILE)
            for m in range(8):
                pool.wait_ge(emptied["dve"], emptied_by("dve", NUM[f"ga{m}"]))
                pool.tensor_tensor(t1[m % 2], t1[m % 2], sgs[:, m, :], ALU.mult).then_inc(gated, 1)
                pool.wait_ge(gated, m + 1)
                pool.wait_ge(emptied["dve"], emptied_by("dve", NUM[f"po{m}"]))
                pool.tensor_tensor(m_t[:, m, :], t1[m % 2], t2[m % 2], ALU.add).then_inc(merged, 1)
            pool.wait_ge(rows_zeroed, 16 * ZEROED)
            pool.wait_ge(rows_ready, 1)
            for i in range(TT):
                for k in range(2):
                    pool.indirect_dma_start(
                        out=x_rows, out_offset=bass.IndirectOffsetOnAxis(ap=rows_i[:ROWS[i], i, k:k + 1], axis=0),
                        in_=xn2[:ROWS[i], i, :], in_offset=None).then_inc(scattered, 16)

            pool.sem_inc(y_free, 1)
            with pool.Fori(0, NE) as e:
                pool.wait_ge(y_ready, e + 1)
                pool.dma_start(y_rows[bass.ds(e * TILE, TILE), :], y_sb).then_inc(y_stored, 16)
                pool.wait_ge(y_stored, e * 16 + 16)
                pool.sem_inc(y_free, 1)
            pool.wait_ge(counts_ready, 1)
            pool.sem_inc(ov_done, 1)

            def more(i, row, n):
                pool.wait_ge(y_ready, n + NE)
                pool.dma_start(y_rows[bass.ds(row, TILE), :], y_sb).then_inc(y_stored, 16)
                pool.wait_ge(y_stored, (n + NE) * 16)
                pool.sem_inc(y_free, 1)
                pool.sem_inc(ov_done, 1)

            overflow(pool, more)
            for i in range(TT):
                for k in range(2):
                    pool.indirect_dma_start(
                        out=at((2 * i + k) * D, D, ROWS[i]), out_offset=None, in_=y_rows,
                        in_offset=bass.IndirectOffsetOnAxis(ap=rows_i[:ROWS[i], i, k:k + 1], axis=0),
                    ).then_inc(gathered[i], 16)

        @block.scalar
        def _(act):
            def load(dst, src, s):
                act.dma_start(dst, src).then_inc(s, 16)

            def emptying(ins):
                ins.then_inc(emptied["act"], 1)

            load(g_b, a["g_mix"][0:1].to_broadcast((P, D)), g_in)
            par_dst = [(0, "ssm_a_re"), (16, "ssm_a_im"), (32, "state_ssm_re"), (48, "state_ssm_im")]
            for r, name in par_dst:
                src = a[name][0] if name[:3] == "ssm" else a[name][0, 0]
                load(par_rows[r:r + 16, :], src.rearrange("(j g) n -> j (g n)", g=2), small_in)
            load(dt_rows, a["ssm_log_dt"][0].rearrange("(j g) -> j g", g=2), small_in)
            load(par_rows[80:84, :], a["ssm_d"][0].rearrange("(b g) q -> b (g q)", b=4), small_in)
            load(par_rows[84:92, :], a["pool_scale"][0].rearrange("(m p) -> m p", p=P), small_in)
            load(cache_rows, a["cache_pool"][0, 0], small_in)
            for r, name in enumerate(("ssm_b_re", "ssm_b_im")):
                load(b_in[:, r], a[name][0].rearrange("(j g) n q -> (g n) j q", g=2), b_loaded)
            for r, name in enumerate(("ssm_c_re", "ssm_c_im")):
                src = a[name][0].rearrange("(h j g) q n -> g h j q n", h=2, g=2)
                dst = c_in.rearrange("p (r h g n) -> p r h g n", r=2, h=2, g=2)
                for hh in range(2):
                    for g in range(2):
                        load(dst[:, r, hh, g, :], src[g, hh], c_loaded)
            load(w_r[:, :, 0:4], a["w_router_group"][0].rearrange("(k p) n -> p k n", p=P), wr_in)
            load(w_r[:, :, 4:36], a["w_router_expert"][0].rearrange("(k p) g e -> p k (g e)", p=P), wr_in)
            act.wait_ge(ss_ready, 1)
            act.wait_ge(x_in, 16 * TT)
            for i in range(TT):
                if i:
                    act.wait_ge(squares, i)
                act.activation(junk0[:ROWS[i]], x_tok[:ROWS[i], i, :], ACT.Square,
                               accum_out=ss[:ROWS[i], i:i + 1]).then_inc(squares, 1)
            act.wait_ge(mean_sq, 1)
            act.activation(rstd, ss, ACT.Sqrt).then_inc(root, 1)
            for i in range(TT):
                psum_waits(act, f"xt{i}")
                r = ROWS[i]
                src = pair(NUM[f"xt{i}"]).rearrange("p h (k t) -> p (h k) t", k=4)
                emptying(act.activation(xn_t[:, :, i * P:i * P + r], src[:, :, 0:r], ACT.Copy))

            def halves(ap):
                return ap.rearrange("p (h t) -> p h t", h=2)

            def evacuate(name, dst, func):
                psum_waits(act, name)
                emptying(act.activation(halves(dst), pair(NUM[name])[:, :, 0:HALF], func))

            for m in range(4):
                evacuate(f"u{m}", u_t[:, m, :], ACT.Copy)
            for m in range(4):
                evacuate(f"gs{m}", sgs[:, m, :], ACT.Sigmoid)
            for r in range(4):
                psum_waits(act, f"st{r}")
                emptying(act.activation(s_t[:, r * 1024:(r + 1) * 1024].rearrange("p (h n) -> p h n", h=2),
                                        pair(NUM[f"st{r}"]), ACT.Copy))
            for r in range(4):
                psum_waits(act, f"usq{r}")
                emptying(act.activation(usq[:, r * 8 * NC:(r + 1) * 8 * NC].rearrange("p (h n) -> p h n", h=2),
                                        pair(NUM[f"usq{r}"])[:, :, 0:4 * NC], ACT.Copy))
            for m in range(4, 8):
                evacuate(f"gs{m}", sgs[:, m, :], ACT.Sigmoid)
            for r in range(4):
                psum_waits(act, f"y{r}")
                dst = gc[0:NC].rearrange("c (t b g q) -> c b g t q", t=L, b=4, g=8)[:, r]
                src = pair(NUM[f"y{r}"])[0:NC].rearrange("c h (g t q) -> c (h g) t q", g=4, t=L)
                emptying(act.activation(dst, src, ACT.Gelu_apprx_tanh))
            for m in range(4):
                psum_waits(act, f"up{m}")
                src = pair(NUM[f"up{m}"])
                act.activation(up_t[:, m, HIST:HIST + HALF], src[:, 0, 0:HALF], ACT.Copy)
                act.activation(up_t[:, m, HIST + HALF:HIST + SEQ], src[:, 1, 0:SEQ - HALF], ACT.Copy)
                emptying(act.activation(up_t[:, m, 2 * HIST + SEQ:UPW], src[:, 1, SEQ - HALF:HALF], ACT.Copy))
            psum_waits(act, "hist")
            emptying(act.activation(hist_rows.rearrange("p (s n) -> p s n", s=2), pair(NUM["hist"])[0:HIST], ACT.Copy))
            psum_waits(act, "gt3")
            for m in range(8):
                evacuate(f"gp{m}", sgp[:, m, :], ACT.Sigmoid)
            for m in range(8):
                psum_waits(act, f"gb{m}")
                if m >= 2:
                    act.wait_ge(emptied["dve"], emptied_by("dve", NUM[f"ga{m - 2}"]))
                act.activation(halves(sig_b[m % 2]), pair(NUM[f"gb{m}"])[:, :, 0:HALF], ACT.Sigmoid)\
                    .then_inc(emptied["act"], 1)
            act.wait_ge(xn_ready, TT)
            load(g_b, a["g_ffn"][0:1].to_broadcast((P, D)), g_in)

            def norm2(i):
                act.wait_ge(emptied["dve"], emptied_by("dve", NUM[f"out{i}"]))
                if i:
                    act.wait_ge(squares2, i)
                act.activation(junk1[:ROWS[i]], x_tok[:ROWS[i], i, :], ACT.Square,
                               accum_out=ss[:ROWS[i], i:i + 1]).then_inc(squares2, 1)
                act.wait_ge(mean2, i + 1)
                act.activation(rstd[:ROWS[i], i:i + 1], ss[:ROWS[i], i:i + 1], ACT.Sqrt).then_inc(root2, 1)

            def x2t(i):
                psum_waits(act, f"x2t{i}")
                r = ROWS[i]
                src = pair(NUM[f"x2t{i}"]).rearrange("p h (k t) -> p (h k) t", k=4)
                emptying(act.activation(xn2_t[:, :, i * P:i * P + r], src[:, :, 0:r], ACT.Copy))

            norm2(0)
            for i in range(TT):
                if i + 1 < TT:
                    norm2(i + 1)
                x2t(i)
            act.wait_ge(xn2_ready, TT)
            load(g_b, a["g_final"].rearrange("(o d) -> o d", o=1).to_broadcast((P, D)), g_in)
            act.wait_ge(neg_ready, 1)
            act.activation(g_exp, g_exp, ACT.Exp).then_inc(exp_ready, 1)
            act.wait_ge(neg_ready, 2)
            act.activation(e_neg, e_neg, ACT.Exp).then_inc(exp_ready, 1)

            def high(hi, c, arrival):
                act.wait_ge(w_in[c], 16 * arrival)
                act.activation(hi, chunk(c), ACT.Copy).then_inc(hi_ready, 1)

            def rows_out(e, n, used):
                act.wait_ge(w_used, used)
                act.activation(gu_rows[:, n * F:(n + 1) * F], ps[0:PAIR, 2 + n, :], ACT.Copy).then_inc(gu_ready, 1)

            def gate(e):
                act.wait_ge(folded, 2 * e + 2)
                act.activation(silu, ps[:, 4, 0:4 * TILE], ACT.Silu).then_inc(silu_ready, 1)

            def h_high(e):
                act.wait_ge(h_ready, e + 1)
                act.activation(h_split.rearrange("p (k t) -> p k t", k=4)[:, :, 0:TILE],
                               h.rearrange("p (k t) -> p k t", k=4), ACT.Copy).then_inc(h_hi_ready, 1)

            def x_high(e, par):
                act.wait_ge(xt_done, e + 1)
                act.activation(x_split[par].rearrange("p (h k t) -> p h k t", h=2, k=4)[:, :, :, 0:TILE],
                               ps[:, 0:2, 0:4 * TILE].rearrange("p h (k t) -> p h k t", k=4),
                               ACT.Copy).then_inc(x_hi_ready, 1)

            def y_low(used):
                act.wait_ge(w_used, used)
                act.activation(y_lo.rearrange("p (h n) -> p h n", h=2), ps[TILE:PAIR, 6:8, :],
                               ACT.Copy).then_inc(y_lo_ready, 1)

            def stage(e, par, first=False, second=False, final=False):
                def next_high(c):
                    if not first:
                        act.wait_ge(w_used, number(e, c - 2))
                    elif c == 3:
                        act.wait_ge(w_used, 1)
                    high(parts_of(c, first)[0], c, e + 1 if c < 4 else e)

                next_high(0)
                if not first and not second:
                    y_low(number(e, 0))
                next_high(1)
                if not first:
                    gate(e - 1)
                next_high(2)
                if not first:
                    h_high(e - 1)
                next_high(3)
                if not final:
                    x_high(e + 1, 1 - par)
                rows_out(e, 0, number(e, 2, first))
                if not first:
                    next_high(4)
                rows_out(e, 1, number(e, 4, first))
                if not first:
                    next_high(5)

            x_high(0, 0)
            stage(0, 0, first=True)
            stage(1, 1, second=True)
            with act.Fori(1, NE // 2 - 1) as i:
                for par in range(2):
                    stage(2 * i + par, par)
            stage(NE - 2, 0)
            stage(NE - 1, 1, final=True)
            y_low(6 * NE - 2)
            gate(NE - 1)
            h_high(NE - 1)
            for c in (4, 5):
                act.wait_ge(w_used, 6 * NE - 8 + c)
                high(w_hi[c % 3], c, NE)
            y_low(6 * NE)
            act.wait_ge(counts_ready, 1)

            def more(i, row, n):
                e = n + (NE - 1)
                act.wait_ge(ov_done, n)
                x_high(e, 0)
                for c in range(6):
                    if c >= 3:
                        act.wait_ge(w_used, 6 * e + (c - 2))
                    high(w_hi[c % 3], c, n + NE)
                for k in range(2):
                    rows_out(e, k, 6 * e + (2 * k + 2))
                gate(e)
                h_high(e)
                y_low(6 * e + 6)

            overflow(act, more)
            for i in range(TT):
                act.wait_ge(sum_ready, i + 1)
                act.activation(at(10 * D + i * D, D, ROWS[i]), x_tok[:ROWS[i], i, :], ACT.Square,
                               accum_out=ss[:ROWS[i], i:i + 1]).then_inc(squares3, 1)
                act.wait_ge(mean3, i + 1)
                act.activation(rstd[:ROWS[i], i:i + 1], ss[:ROWS[i], i:i + 1], ACT.Sqrt).then_inc(root3, 1)

        @block.vector
        def _(dve):
            done = [0]

            def step(ins):
                done[0] += 1
                ins.then_inc(step_dve, 1)
                dve.wait_ge(step_dve, done[0])

            def tt(out_, x0, x1, op):
                step(dve.tensor_tensor(out_, x0, x1, op))

            def ts(out_, x0, s0, op0, s1=None, op1=None):
                if op1 is None:
                    step(dve.tensor_scalar(out_, x0, s0, None, op0))
                else:
                    step(dve.tensor_scalar(out_, x0, s0, s1, op0, op1))

            def stt(out_, x0, s0, x1, op0, op1):
                step(dve.scalar_tensor_tensor(out=out_, in0=x0, scalar=s0, in1=x1, op0=op0, op1=op1))

            def inverse_root(mean, r):
                tmp = misc(M_SS + 16, TT)[0:r.shape[0], 0:r.shape[1]]
                step(dve.reciprocal(r, r))
                tt(tmp, r, r, ALU.mult)
                tt(tmp, tmp, mean, ALU.mult)
                ts(tmp, tmp, -0.5, ALU.mult, 1.5, ALU.add)
                tt(r, r, tmp, ALU.mult)

            taken = [0]

            def empty(ins, read=False):
                taken[0] += 1
                ins.then_inc(emptied["dve"], 1)
                if read:
                    dve.wait_ge(emptied["dve"], taken[0])

            step(dve.memset(ss, 1.0))
            dve.memset(rstd, 1.0).then_inc(ss_ready, 1)
            dve.wait_ge(small_in, 16 * 8)
            for g in range(2):
                dve.tensor_copy(par_rows[64:80, g * N:(g + 1) * N],
                                dt_rows[:, g:g + 1].to_broadcast((NJ, N))).then_inc(dt_ready, 1)
            dve.wait_ge(squares, TT)
            dve.tensor_scalar(ss, ss, 1.0 / D, EPS, ALU.mult, ALU.add).then_inc(mean_sq, 1)
            dve.wait_ge(mean_sq, 1)
            dve.wait_ge(root, 1)
            inverse_root(ss, rstd)
            dve.wait_ge(g_in, 16)
            for i in range(TT):
                if i >= 2:
                    psum_waits(dve, f"xt{i - 2}")
                r = ROWS[i]
                dve.scalar_tensor_tensor(out=xn_row[i % 2][:r], in0=x_tok[:r, i, :], scalar=rstd[:r, i:i + 1],
                                         in1=g_b[:r], op0=ALU.mult, op1=ALU.mult).then_inc(xn_ready, 1)

            psum_waits(dve, "par")
            pp = pair(NUM["par"])
            step(dve.tensor_copy(prm, pp[:, 0, 0:92]))
            step(dve.tensor_copy(hist_t.rearrange("p g c -> p (g c)"), pp[:, 0, 128:188]))
            empty(dve.tensor_copy(c_t.rearrange("p r j q -> p (r j q)"), pp[:, 1, :]), read=True)
            col = lambda n: misc(M_TMP + 16 * n, 16)
            a_re, a_im, log_dt, d_col = prm[:, 0:16], prm[:, 16:32], prm[:, 64:80], prm[:, 80:84]

            def exp(dst, z, k, r, ki):
                ts(dst, z, 87.0, ALU.min, -87.0, ALU.max)
                ts(k, dst, 1.4426950408889634, ALU.mult, 12582912.0, ALU.add)
                ts(k, k, -12582912.0, ALU.add)
                stt(r, k, -0.693145751953125, dst, ALU.mult, ALU.add)
                stt(r, k, -1.42860677e-06, r, ALU.mult, ALU.add)
                ts(k, k, 127.0, ALU.add)
                step(dve.tensor_copy(ki.bitcast(I32), k))
                ts(ki.bitcast(I32), ki.bitcast(I32), 23, ALU.logical_shift_left)
                ts(dst, r, 1.0 / 5040, ALU.mult)
                for c in (1.0 / 720, 1.0 / 120, 1.0 / 24, 1.0 / 6, 0.5, 1.0):
                    stt(dst, dst, c, r, ALU.add, ALU.mult)
                ts(dst, dst, 1.0, ALU.add)
                tt(dst, dst, ki, ALU.mult)

            dt, lr, mag, ang, s1, s2 = col(0), col(1), col(2), col(3), col(4), col(5)
            t_a, t_b, t_c = col(6), col(7), col(8)
            exp(dt, log_dt, t_a, t_b, t_c)
            ts(lr, a_re, -1e-4, ALU.min)
            tt(s1, lr, dt, ALU.mult)
            exp(mag, s1, t_a, t_b, t_c)
            tt(ang, a_im, dt, ALU.mult)
            ts(t_a, ang, 0.15915494309189535, ALU.mult, 12582912.0, ALU.add)
            ts(t_a, t_a, -12582912.0, ALU.add)
            for c in (6.28125, 0.0019340515136718750, 1.2556659146547282e-06):
                stt(ang, t_a, -c, ang, ALU.mult, ALU.add)
            ts(ang, ang, 0.5, ALU.mult)
            tt(t_a, ang, ang, ALU.mult)
            sin_c = (-1.0 / 39916800, 1.0 / 362880, -1.0 / 5040, 1.0 / 120, -1.0 / 6)
            ts(s1, t_a, 1.0 / 6227020800, ALU.mult)
            for c in sin_c:
                stt(s1, s1, c, t_a, ALU.add, ALU.mult)
            stt(s1, s1, 1.0, ang, ALU.add, ALU.mult)
            cos_c = (1.0 / 479001600, -1.0 / 3628800, 1.0 / 40320, -1.0 / 720, 1.0 / 24, -0.5)
            ts(s2, t_a, -1.0 / 87178291200, ALU.mult)
            for c in cos_c:
                stt(s2, s2, c, t_a, ALU.add, ALU.mult)
            ts(s2, s2, 1.0, ALU.add)
            tt(t_b, s1, s2, ALU.mult)
            stt(t_b, t_b, 2.0, mag, ALU.mult, ALU.mult)
            tt(t_a, s1, s1, ALU.mult)
            ts(t_a, t_a, -2.0, ALU.mult, 1.0, ALU.add)
            tt(t_a, t_a, mag, ALU.mult)
            pre, pim = powers[:, 0], powers[:, 1]
            step(dve.memset(pre[:, 0], 1.0))
            step(dve.memset(pim[:, 0], 0.0))
            step(dve.tensor_copy(pre[:, 1], t_a))
            step(dve.tensor_copy(pim[:, 1], t_b))

            def cmul(dr, di, ar, ai, br, bi, t, ready=None):
                tt(dr, ar, br, ALU.mult)
                tt(t, ai, bi, ALU.mult)
                tt(dr, dr, t, ALU.subtract)
                tt(di, ar, bi, ALU.mult)
                tt(t, ai, br, ALU.mult)
                if ready is None:
                    tt(di, di, t, ALU.add)
                else:
                    dve.tensor_tensor(di, di, t, ALU.add).then_inc(ready, 1)

            for k in (1, 2, 4):
                shape = (P, k, NJ)
                tmp = misc(M_TMP + 320, k * NJ).rearrange("p (t j) -> p t j", t=k)
                cmul(pre[:, k + 1:2 * k + 1], pim[:, k + 1:2 * k + 1], pre[:, 1:k + 1], pim[:, 1:k + 1],
                     pre[:, k:k + 1].to_broadcast(shape), pim[:, k:k + 1].to_broadcast(shape), tmp)
            step(dve.tensor_copy(a4[:, :, 0, 0], pre[:, 8]))
            step(dve.tensor_copy(a4[:, :, 1, 1], pre[:, 8]))
            step(dve.tensor_copy(a4[:, :, 1, 0], pim[:, 8]))
            ts(a4[:, :, 0, 1], pim[:, 8], -1.0, ALU.mult)
            num, den, k_re, k_im = col(9), col(10), col(11), col(12)
            ts(num, t_a, -1.0, ALU.add)
            tt(den, lr, lr, ALU.mult)
            tt(s1, a_im, a_im, ALU.mult)
            tt(den, den, s1, ALU.add)
            step(dve.reciprocal(den, den))
            tt(k_re, num, lr, ALU.mult)
            tt(s1, t_b, a_im, ALU.mult)
            tt(k_re, k_re, s1, ALU.add)
            tt(k_re, k_re, den, ALU.mult)
            tt(k_im, t_b, lr, ALU.mult)
            tt(s1, num, a_im, ALU.mult)
            tt(k_im, k_im, s1, ALU.subtract)
            tt(k_im, k_im, den, ALU.mult)
            dve.wait_ge(b_loaded, 32)
            wide = (P, NJ, Q)
            tmp = prod[:, 0:256].rearrange("p (j q) -> p j q", j=NJ)
            cmul(bbar[:, 0], bbar[:, 1], k_re.unsqueeze(2).to_broadcast(wide), k_im.unsqueeze(2).to_broadcast(wide),
                 b_in[:, 0], b_in[:, 1], tmp)
            dve.wait_ge(toep_zero, 1)
            bb = bbd.rearrange("p (j r g q) -> p r j g q", j=NJ, r=2, g=2)
            for r in range(2):
                for g in range(2):
                    dve.tensor_copy(bb[64 * g:64 * g + 64, r, :, g, :], bbar[64 * g:64 * g + 64, r])\
                        .then_inc(bbd_ready, 1)
            big = (P, NJ, 9, Q)
            cp = [c.rearrange("p (j t q) -> p j t q", j=NJ, t=9) for c in cpow]
            tmp = prod.rearrange("p (j t q) -> p j t q", j=NJ, t=9)
            c_b = [c_t[:, r].unsqueeze(2).to_broadcast(big) for r in range(2)]
            p_b = [x.rearrange("p t j -> p j t").unsqueeze(3).to_broadcast(big) for x in (pre, pim)]
            tt(cp[0], c_b[0], p_b[0], ALU.mult)
            tt(tmp, c_b[1], p_b[1], ALU.mult)
            tt(cp[0], cp[0], tmp, ALU.subtract)
            tt(cp[1], c_b[0], p_b[1], ALU.mult)
            tt(tmp, c_b[1], p_b[0], ALU.mult)
            dve.scalar_tensor_tensor(out=cp[1], in0=cp[1], scalar=-1.0, in1=tmp, op0=ALU.mult, op1=ALU.subtract)\
                .then_inc(cpow_ready, 1)
            sn = s_nat.rearrange("p (j r s q) -> p r s j q", j=NJ, r=2, s=L)
            tmp = prod[:, 0:256].rearrange("p (j q) -> p j q", j=NJ)
            for s in range(L):
                p_re = pre[:, 7 - s].unsqueeze(2).to_broadcast(wide)
                p_im = pim[:, 7 - s].unsqueeze(2).to_broadcast(wide)
                cmul(sn[:, 0, s], sn[:, 1, s], p_re, p_im, bbar[:, 0], bbar[:, 1], tmp,
                     s_ready if s == L - 1 else None)

            psum_waits(dve, "kt")
            empty(dve.tensor_copy(k_sb, pair(NUM["kt"])[:, 0, :]), read=True)
            for b in range(4):
                lag0 = k_sb[:, b * P:b * P + Q]
                dve.scalar_tensor_tensor(out=lag0, in0=diag16, scalar=d_col[:, b:b + 1], in1=lag0,
                                         op0=ALU.mult, op1=ALU.add).then_inc(taps_ready, 1)
            dve.wait_ge(rows_zeroed, 16 * ZEROED)
            for r in range(4):
                psum_waits(dve, f"uc{r}")
                empty(dve.tensor_copy(uc[0:NC].rearrange("c (g s q) -> c s g q", s=L, g=G)[:, 2 * r:2 * r + 2],
                                      pair(NUM[f"uc{r}"])[0:NC].rearrange("c h (g q) -> c h g q", g=G)))
            dve.wait_ge(taps_out, 16)
            for r in range(3):
                psum_waits(dve, f"v{r}")
                for b in range(2):
                    n = min(3, NJ - (6 * r + 3 * b))
                    copied = dve.tensor_copy(v_all[:, (6 * r + 3 * b) * 2 * NC:(6 * r + 3 * b + n) * 2 * NC],
                                             pair(NUM[f"v{r}"])[:, b, 0:n * 2 * NC])
                    if b == 0:
                        step(copied)
                    else:
                        empty(copied, read=True)
            four = (P, NJ, 2, 2)

            def before_sample():
                return prm[:, 32:64].rearrange("p (r j) -> p j r", r=2)

            def advance(state, c):
                tt(scan_tmp, a4, state.unsqueeze(2).to_broadcast(four), ALU.mult)
                step(dve.tensor_reduce(scan_red, scan_tmp, X, ALU.add))
                tt(v[:, :, :, c], v[:, :, :, c], scan_red, ALU.add)

            advance(before_sample(), PC)
            for c in range(PC + 1, NC):
                advance(v[:, :, :, c - 1], c)
            with dve.Fori(1, PC) as c:
                prev = v[:, :, :, bass.ds(c - 1, 1)].rearrange("p j r c -> p j (r c)")
                here = v[:, :, :, bass.ds(c, 1)].rearrange("p j r c -> p j (r c)")
                dve.tensor_tensor(scan_tmp, a4, prev.unsqueeze(2).to_broadcast(four), ALU.mult).then_inc(scan_step, 1)
                dve.wait_ge(scan_step, c * 3 - 2)
                dve.tensor_reduce(scan_red, scan_tmp, X, ALU.add).then_inc(scan_step, 1)
                dve.wait_ge(scan_step, c * 3 - 1)
                dve.tensor_tensor(here, here, scan_red, ALU.add).then_inc(scan_step, 1)
                dve.wait_ge(scan_step, c * 3)
            dve.wait_ge(hpad_zero, 1)
            for g in range(2):
                row = slice(64 * g, 64 * g + 64)
                dve.tensor_copy(hpad[row, :, :, g, 1:PC], v[row, :, :, 0:PC - 1]).then_inc(hpad_ready, 1)
                dve.tensor_copy(hpad[row, :, :, g, PC], before_sample()[row]).then_inc(hpad_ready, 1)
                dve.tensor_copy(hpad[row, :, :, g, PC + 1:NC], v[row, :, :, PC:NC - 1]).then_inc(hpad_ready, 1)
            fc = fin_cols.rearrange("p (s r j) -> p s j r", s=2, r=2)
            dve.tensor_copy(fc[:, 0], v[:, :, :, PC - 1]).then_inc(fin_ready, 1)
            dve.tensor_copy(fc[:, 1], v[:, :, :, NC - 1]).then_inc(fin_ready, 1)
            for b in range(4):
                psum_waits(dve, f"gt{b}")
                dst = g_t[:, b, :].rearrange("p (c t) -> p t c", t=L)
                src = pair(NUM[f"gt{b}"])
                dve.tensor_copy(dst[:, 0:4], src[:, 0, 0:4 * NC].rearrange("p (t c) -> p t c", t=4))
                empty(dve.tensor_copy(dst[:, 4:8], src[:, 1, 0:4 * NC].rearrange("p (t c) -> p t c", t=4)))
            psum_waits(dve, "fin")
            empty(dve.tensor_copy(fin_rows, pair(NUM["fin"])[0:64, 0, 0:P]))

            def halves(ap):
                return ap.rearrange("p (h t) -> p h t", h=2)

            for m in range(8):
                psum_waits(dve, f"ga{m}")
                dve.wait_ge(emptied["act"], emptied_by("act", NUM[f"gb{m}"]))
                if m >= 2:
                    dve.wait_ge(merged, m - 1)
                empty(dve.tensor_tensor(halves(t1[m % 2]), pair(NUM[f"ga{m}"])[:, :, 0:HALF], halves(sig_b[m % 2]),
                                        ALU.mult))
                psum_waits(dve, f"po{m}")
                empty(dve.scalar_tensor_tensor(out=halves(t2[m % 2]), in0=pair(NUM[f"po{m}"])[:, :, 0:HALF],
                                               scalar=prm[:, 84 + m:85 + m], in1=halves(sgp[:, m, :]),
                                               op0=ALU.mult, op1=ALU.mult))
            for i in range(TT):
                psum_waits(dve, f"out{i}")
                r = ROWS[i]
                x_i = x_tok[:r, i, :].rearrange("p (h n) -> p h n", h=2)
                empty(dve.tensor_tensor(x_i, pair(NUM[f"out{i}"])[:r], x_i, ALU.add), read=True)
                dve.wait_ge(squares2, i + 1)
                mean, root_i = ss[:r, i:i + 1], rstd[:r, i:i + 1]
                dve.tensor_scalar(mean, mean, 1.0 / D, EPS, ALU.mult, ALU.add).then_inc(mean2, 1)
                dve.wait_ge(mean2, i + 1)
                dve.wait_ge(root2, i + 1)
                inverse_root(mean, root_i)
                dve.wait_ge(g_in, 32)
                dve.scalar_tensor_tensor(out=xn2[:r, i, :], in0=x_tok[:r, i, :], scalar=root_i, in1=g_b[:r],
                                         op0=ALU.mult, op1=ALU.mult).then_inc(xn2_ready, 1)
            dve.wait_ge(outs_done, 16 * 6)
            step(dve.memset(logits, 0.0))
            step(dve.tensor_copy(prefer, misc(M_EB, 8)))
            ts(prefer, prefer, -1.0 / TILE, ALU.mult, float(EI), ALU.add)
            psum_waits(dve, "lg")
            lg_ps = pair(NUM["lg"])[:, 0, 0:TT * 36].rearrange("p (i n) -> p i n", i=TT)
            step(dve.tensor_copy(logits[:, 0:4], lg_ps[:, 0:4]))
            empty(dve.tensor_copy(logits[:32, 4], lg_ps[:32, 4]), read=True)
            lg, le = logits[:, :, 0:EG], logits[:, :, EG:36]

            def first_max(hot, vals, best, rank, n):
                full = (P, TT, n)
                step(dve.tensor_reduce(best, vals, X, ALU.max))
                tt(hot, vals, best.unsqueeze(2).to_broadcast(full), ALU.is_equal)
                tt(hot, hot, rank.unsqueeze(1).to_broadcast(full), ALU.mult)
                step(dve.tensor_reduce(s_d, hot, X, ALU.max))
                tt(hot, hot, s_d.unsqueeze(2).to_broadcast(full), ALU.is_equal)

            first_max(g_hot, lg, s_a, prefer[:, 0:EG], EG)
            dve.tensor_tensor(g_exp, lg, s_a.unsqueeze(2).to_broadcast((P, TT, EG)), ALU.subtract)\
                .then_inc(neg_ready, 1)
            tt(le_mul, le.rearrange("p i (g e) -> p i g e", g=EG), g_hot.unsqueeze(3).to_broadcast((P, TT, EG, EI)),
               ALU.mult)
            step(dve.tensor_reduce(le_sel, le_mul.rearrange("p i g e -> p i e g"), X, ALU.add))
            first_max(i_hot[0], le_sel, s_b, prefer, EI)
            stt(i_tmp, i_hot[0], -BIG, le_sel, ALU.mult, ALU.add)
            first_max(i_hot[1], i_tmp, s_c, prefer, EI)
            dve.tensor_tensor(e_neg, s_c, s_b, ALU.subtract).then_inc(neg_ready, 1)
            for k in range(2):
                hot = onehot[k].rearrange("p i (g e) -> p i g e", g=EG)
                tt(hot, g_hot.unsqueeze(3).to_broadcast((P, TT, EG, EI)),
                   i_hot[k].unsqueeze(2).to_broadcast((P, TT, EG, EI)), ALU.mult)
            dve.tensor_tensor(chosen, onehot[0], onehot[1], ALU.add).then_inc(chosen_ready, 1)
            dve.wait_ge(exp_ready, 2)
            step(dve.tensor_reduce(s_a, g_exp, X, ALU.add))
            ts(s_b, e_neg, 1.0, ALU.add)
            tt(s_a, s_a, s_b, ALU.mult)
            step(dve.reciprocal(weight[:, :, 0], s_a))
            tt(weight[:, :, 1], weight[:, :, 0], e_neg, ALU.mult)
            psum_waits(dve, "rank")
            rk = pair(NUM["rank"])
            step(dve.tensor_copy(ranks[:, 0:4], rk[:, 0, 0:4 * NE].rearrange("p (i n) -> p i n", i=4)))
            step(dve.memset(rows_f, 0.0))
            step(dve.memset(ranks[:, 4], 0.0))
            step(dve.tensor_copy(ranks[:32, 4], rk[:32, 0, 4 * NE:5 * NE]))
            empty(dve.tensor_copy(counts, rk[:, 1, 0:NE]), read=True)
            full = (P, TT, NE)
            beyond, first = small(NE), [small(NE), small(NE)]
            ts(beyond, counts, -float(TILE), ALU.add, 0.0, ALU.max)
            step(dve.memset(first[0][:, 0:1], 0.0))
            step(dve.tensor_copy(first[0][:, 1:NE], beyond[:, 0:NE - 1]))
            shift, n = 1, 0
            while shift < NE:
                src, dst = first[n % 2], first[(n + 1) % 2]
                step(dve.tensor_copy(dst[:, 0:shift], src[:, 0:shift]))
                tt(dst[:, shift:NE], src[:, shift:NE], src[:, 0:NE - shift], ALU.add)
                shift, n = 2 * shift, n + 1
            first, other = first[n % 2], first[(n + 1) % 2]
            ts(first, first, float(MAIN), ALU.add)
            ts(other, first, -float(TILE), ALU.add)
            tt(other, other, ebase, ALU.subtract)
            ts(rank_mul, ranks, float(TILE), ALU.is_ge)
            tt(rank_mul, rank_mul, other.unsqueeze(1).to_broadcast(full), ALU.mult)
            tt(ranks, ranks, ebase.unsqueeze(1).to_broadcast(full), ALU.add)
            tt(ranks, ranks, rank_mul, ALU.add)
            for k in range(2):
                tt(rank_mul, ranks, onehot[k], ALU.mult)
                step(dve.tensor_reduce(rows_f[:, :, k], rank_mul, X, ALU.add))
            dve.tensor_copy(rows_i, rows_f).then_inc(rows_ready, 1)
            for j in range(EXTRA):
                ts(tab_f[0:1, 0, j], counts[0:1], float(TILE * (j + 1)), ALU.is_gt)
                ts(tab_f[0:1, 1, j], first[0:1], float(TILE * j), ALU.add)
                ts(tab_f[0:1, 1, j], tab_f[0:1, 1, j], float(NROWS - TILE), ALU.min)
            step(dve.tensor_copy(table[:, 0:2 * NE * EXTRA].rearrange("p (a e j) -> p a j e", a=2, j=EXTRA),
                                 tab_f[0:1]))
            step(dve.tensor_reduce(s_a[0:1, 0:1], counts[0:1], X, ALU.max))
            ts(s_a[0:1, 0:1], s_a[0:1, 0:1], float(TILE), ALU.is_gt)
            dve.tensor_copy(table[:, 2 * NE * EXTRA:2 * NE * EXTRA + 1], s_a[0:1, 0:1]).then_inc(counts_ready, 1)
            dve.wait_ge(counts_ready, 1)

            def low(hi, lo, c, n):
                dve.wait_ge(hi_ready, n + 1)
                dve.tensor_tensor(lo, chunk(c), hi.bitcast(F32), ALU.subtract).then_inc(lo_ready, 1)

            def hidden(e):
                dve.wait_ge(silu_ready, e + 1)
                dve.tensor_tensor(h, ps[:, 4, 4 * TILE:8 * TILE], silu, ALU.mult).then_inc(h_ready, 1)

            def h_low(e):
                dve.wait_ge(h_hi_ready, e + 1)
                dve.wait_ge(h_ready, e + 1)
                parts = h_split.rearrange("p (k t) -> p k t", k=4)
                dve.tensor_tensor(parts[:, :, TILE:PAIR], h.rearrange("p (k t) -> p k t", k=4),
                                  parts[:, :, 0:TILE].bitcast(F32), ALU.subtract).then_inc(h_lo_ready, 1)

            def x_low(e, par):
                dve.wait_ge(x_hi_ready, e + 1)
                parts = x_split[par].rearrange("p (h k t) -> p h k t", h=2, k=4)
                dve.tensor_tensor(parts[:, :, :, TILE:PAIR], ps[:, 0:2, 0:4 * TILE].rearrange("p h (k t) -> p h k t", k=4),
                                  parts[:, :, :, 0:TILE].bitcast(F32), ALU.subtract).then_inc(x_lo_ready, 1)

            def result(e):
                dve.wait_ge(y_lo_ready, e + 1)
                dve.wait_ge(y_free, e + 1)
                dve.tensor_tensor(y_sb.rearrange("p (h n) -> p h n", h=2), ps[0:TILE, 6:8, :],
                                  y_lo.rearrange("p (h n) -> p h n", h=2), ALU.add).then_inc(y_ready, 1)

            def stage(e, par, first=False, second=False, final=False):
                def next_low(c):
                    low(*parts_of(c, first), c, number(e, c, first))

                next_low(0)
                if not first and not second:
                    result(e - 2)
                next_low(1)
                if not first:
                    hidden(e - 1)
                next_low(2)
                if not first:
                    h_low(e - 1)
                next_low(3)
                if not final:
                    x_low(e + 1, 1 - par)
                if not first:
                    next_low(4)
                    next_low(5)

            x_low(0, 0)
            stage(0, 0, first=True)
            stage(1, 1, second=True)
            with dve.Fori(1, NE // 2 - 1) as i:
                for par in range(2):
                    stage(2 * i + par, par)
            stage(NE - 2, 0)
            stage(NE - 1, 1, final=True)
            result(NE - 2)
            hidden(NE - 1)
            h_low(NE - 1)
            for c in (4, 5):
                low(w_hi[c % 3], w_lo[c % 3], c, 6 * NE - 6 + c)
            result(NE - 1)

            def more(i, row, n):
                e = n + (NE - 1)
                x_low(e, 0)
                for c in range(6):
                    low(w_hi[c % 3], w_lo[c % 3], c, 6 * e + c)
                hidden(e)
                h_low(e)
                result(e)

            overflow(dve, more)
            dve.wait_ge(g_in, 48)
            for i in range(TT):
                r = ROWS[i]
                dve.wait_ge(gathered[i], 32)
                xi = x_tok[:r, i, :]
                stt(xi, at(2 * i * D, D, r), weight[:r, i, 0:1], xi, ALU.mult, ALU.add)
                dve.scalar_tensor_tensor(out=xi, in0=at((2 * i + 1) * D, D, r), scalar=weight[:r, i, 1:2], in1=xi,
                                         op0=ALU.mult, op1=ALU.add).then_inc(sum_ready, 1)
                dve.wait_ge(sum_ready, i + 1)
                dve.wait_ge(squares3, i + 1)
                mean, root_i = ss[:r, i:i + 1], rstd[:r, i:i + 1]
                dve.tensor_scalar(mean, mean, 1.0 / D, EPS, ALU.mult, ALU.add).then_inc(mean3, 1)
                dve.wait_ge(mean3, i + 1)
                dve.wait_ge(root3, i + 1)
                inverse_root(mean, root_i)
                dve.scalar_tensor_tensor(out=xn2[:r, i, :], in0=xi, scalar=root_i, in1=g_b[:r],
                                         op0=ALU.mult, op1=ALU.mult).then_inc(final_ready, 1)

        @block.tensor
        def _(pe):
            def begin(name):
                i = NUM[name]
                if i >= 4:
                    owner = TASKS[i - 4][1]
                    pe.wait_ge(emptied[owner], emptied_by(owner, i - 4))
                return pair(i)

            def end(ins):
                ins.then_inc(psum_ready, 1)

            pe.wait_ge(consts, 1)
            pe.wait_ge(small_in, 16 * 8)
            pe.wait_ge(dt_ready, 2)
            pe.wait_ge(c_loaded, 16 * 8)
            dst = begin("par")
            pe.transpose(dst[:, 0, 0:92], par_rows, ident[0:92, 0:92])
            for g in range(4):
                pe.transpose(dst[:, 0, 128 + 15 * g:143 + 15 * g], cache_rows[:, g * P:(g + 1) * P],
                             ident[0:HIST, 0:HIST])
            for n in range(4):
                last = pe.transpose(dst[:, 1, n * P:(n + 1) * P], c_in[:, n * P:(n + 1) * P], ident)
            end(last)
            for i in range(TT):
                dst, r = begin(f"xt{i}"), ROWS[i]
                pe.wait_ge(xn_ready, i + 1)
                for k in range(KD):
                    last = pe.transpose(dst[:, k // 4, (k % 4) * P:(k % 4) * P + r],
                                        xn_row[i % 2][:r, k * P:(k + 1) * P], ident[0:r, 0:r])
                end(last)
            pe.wait_ge(emptied["act"], emptied_by("act", NUM["xt4"]))

            def project(name, w, rhs, m, kk):
                dst = begin(name)
                for hh in range(2):
                    for k in range(kk):
                        last = pe.matmul(dst[:, hh, 0:HALF], w[:, k, m * P:(m + 1) * P],
                                         rhs[:, k, hh * HALF:(hh + 1) * HALF], start=(k == 0), stop=(k == kk - 1))
                end(last)

            def arrived(b):
                pe.wait_ge(w_stream[b % 2], 16 * (b // 2 + 1))
                return w_slot(b % 2, 4 if b in (6, 7) else 8)

            w = arrived(0)
            for m in range(4):
                project(f"u{m}", w, xn_t, m, KD)
            w = arrived(1)
            for m in range(4):
                project(f"gs{m}", w, xn_t, m, KD)
            dst = begin("kt")
            pe.wait_ge(bbd_ready, 4)
            pe.wait_ge(cpow_ready, 1)
            for j in range(NJ):
                for r in range(2):
                    last = pe.matmul(dst[32 * (j % 4):32 * (j % 4) + 32, 0, (j // 4) * P:(j // 4 + 1) * P],
                                     bbd[:, (2 * j + r) * 32:(2 * j + r + 1) * 32], cpow[r][:, j * 144:j * 144 + P],
                                     start=(r == 0), stop=(r == 1))
            end(last)
            pe.wait_ge(s_ready, 1)
            for r in range(4):
                dst = begin(f"st{r}")
                for n in range(8):
                    last = pe.transpose(dst[:, n // 4, (n % 4) * P:(n % 4 + 1) * P],
                                        s_nat[:, (8 * r + n) * P:(8 * r + n + 1) * P], ident)
                end(last)
            pe.wait_ge(emptied["act"], emptied_by("act", NUM["u3"]))
            for r in range(4):
                dst = begin(f"uc{r}")
                for hh in range(2):
                    for b in range(4):
                        frames = u_t[:, b, :].rearrange("p (c s) -> p s c", s=L)[:, 2 * r + hh, :]
                        last = pe.transpose(dst[0:NC, hh, b * P:(b + 1) * P], frames, ident)
                end(last)
            pe.wait_ge(emptied["dve"], emptied_by("dve", NUM["uc3"]))
            for r in range(4):
                dst = begin(f"usq{r}")
                for n in range(8):
                    last = pe.transpose(dst[:, n // 4, (n % 4) * NC:(n % 4 + 1) * NC], uc[0:NC, (8 * r + n) * P:(8 * r + n + 1) * P],
                                        ident[0:NC, 0:NC])
                end(last)
            pe.wait_ge(emptied["act"], emptied_by("act", NUM["usq3"]))
            for r in range(3):
                dst = begin(f"v{r}")
                for n in range(min(6, NJ - 6 * r)):
                    j = 6 * r + n
                    for ri in range(2):
                        for g in range(2):
                            o = (2 * (n % 3) + ri) * NC
                            last = pe.matmul(dst[64 * g:64 * g + 64, n // 3, o:o + NC],
                                             s_t[:, (2 * j + ri) * P + 64 * g:(2 * j + ri) * P + 64 * g + 64],
                                             usq[:, (2 * j + g) * NC:(2 * j + g + 1) * NC], start=True, stop=True)
                end(last)
            w = arrived(2)
            for m in range(4):
                project(f"gs{m + 4}", w, xn_t, m, KD)
            pe.wait_ge(toep_in, 16 * L * 4)
            pe.wait_ge(hpad_ready, 6)
            for r in range(4):
                dst = begin(f"y{r}")
                for n in range(8):
                    g = 8 * r + n
                    j, o = g // 2, dst[0:NC, n // 4, (n % 4) * P:(n % 4 + 1) * P]
                    pe.matmul(o, usq[:, g * NC:(g + 1) * NC], toep[:, g * P:(g + 1) * P], start=True, stop=False)
                    for ri in range(2):
                        last = pe.matmul(o, hpad[:, j, ri, g % 2, :], cpow[ri][:, j * 144 + Q:j * 144 + Q + P],
                                         start=False, stop=(ri == 1))
                end(last)
            for b in range(4):
                dst = begin(f"gt{b}")
                if b == 0:
                    pe.wait_ge(emptied["act"], emptied_by("act", NUM["y3"]))
                for t in range(L):
                    last = pe.transpose(dst[:, t // 4, (t % 4) * NC:(t % 4 + 1) * NC],
                                        gc[0:NC, t * 512 + b * P:t * 512 + (b + 1) * P], ident[0:NC, 0:NC])
                end(last)
            dst = begin("fin")
            pe.wait_ge(fin_ready, 2)
            end(pe.transpose(dst[0:64, 0, 0:P], fin_cols, ident))
            w = arrived(3)
            for m in range(4):
                project(f"up{m}", w, xn_t, m, KD)
            dst = begin("hist")
            pe.wait_ge(emptied["act"], emptied_by("act", NUM["up3"]))
            for n, c in enumerate((SEQ, UPW - HIST)):
                for g in range(4):
                    last = pe.transpose(dst[0:HIST, n, g * P:(g + 1) * P], up_t[:, g, c:c + HIST], ident)
            end(last)
            for b in (4, 5):
                w = arrived(b)
                for m in range(4):
                    project(f"gp{m + 4 * (b - 4)}", w, xn_t, m, KD)
            w_a, w_b = arrived(6), arrived(7)
            pe.wait_ge(emptied["dve"], emptied_by("dve", NUM["gt3"]))
            pe.wait_ge(pw_in, 16)
            pe.wait_ge(z_ready, 4)
            for m in range(8):
                project(f"gb{m}", w_b, g_t, m, 4)
                project(f"ga{m}", w_a, g_t, m, 4)
                dst, g = begin(f"po{m}"), m // 2
                for hh in range(2):
                    last = pe.matmul(dst[:, hh, 0:HALF], pool_w[:, g * 256 + (m % 2) * P:g * 256 + (m % 2) * P + P],
                                     z_t[:, g, hh * HALF:(hh + 1) * HALF], start=True, stop=True)
                end(last)
            w0, w1 = arrived(8), arrived(9)
            pe.wait_ge(merged, 8)

            def out_proj(i):
                dst, r = begin(f"out{i}"), ROWS[i]
                for n, wn in enumerate((w0, w1)):
                    for k in range(8):
                        last = pe.matmul(dst[:r, n, :], m_t[:, k, i * P:i * P + r], wn[:, k, :],
                                         start=(k == 0), stop=(k == 7))
                end(last)

            out_proj(0)
            for i in range(TT):
                if i + 1 < TT:
                    out_proj(i + 1)
                dst, r = begin(f"x2t{i}"), ROWS[i]
                pe.wait_ge(xn2_ready, i + 1)
                for k in range(KD):
                    last = pe.transpose(dst[:, k // 4, (k % 4) * P:(k % 4) * P + r],
                                        xn2[:r, i, k * P:(k + 1) * P], ident[0:r, 0:r])
                end(last)
            dst = begin("lg")
            pe.wait_ge(emptied["act"], emptied_by("act", NUM["x2t4"]))
            pe.wait_ge(wr_in, 32)
            for i in range(TT):
                for k in range(KD):
                    last = pe.matmul(dst[:ROWS[i], 0, i * 36:(i + 1) * 36], xn2_t[:, k, i * P:i * P + ROWS[i]],
                                     w_r[:, k, :], start=(k == 0), stop=(k == KD - 1))
            end(last)
            dst = begin("rank")
            pe.wait_ge(chosen_ready, 1)
            pe.wait_ge(consts, 2)
            for i in range(TT):
                r = ROWS[i]
                o = dst[:r, 0, i * NE:(i + 1) * NE]
                for n in range(i):
                    pe.matmul(o, ones[:, :r], chosen[:, n, :], start=(n == 0), stop=False)
                pe.matmul(o, tri[:r, :r], chosen[:r, i, :], start=(i == 0), stop=True)
            for i in range(TT):
                last = pe.matmul(dst[:, 1, 0:NE], ones[:ROWS[i], :], chosen[:ROWS[i], i, :],
                                 start=(i == 0), stop=(i == TT - 1))
            end(last)

            def turn(x, part, s=None):
                for k in range(4):
                    turned = (ps[:, part, k * TILE:(k + 1) * TILE], x[:, (4 * part + k) * P:(4 * part + k + 1) * P],
                              ident[0:TILE, 0:TILE])
                    last = pe.transpose(*turned) if k else pe.matmul(*turned, start=True, stop=True)
                if s is not None:
                    last.then_inc(s, 1)

            def product(hi, lo, xs, c, n):
                pe.wait_ge(lo_ready, n + 1)
                parts = hi, lo
                if c < 4:
                    for k in range(4):
                        kk = 4 * (c % 2) + k
                        for p, w in enumerate(parts):
                            last = pe.matmul(ps[0:PAIR, 2 + c // 2, :], xs[:, kk * PAIR:(kk + 1) * PAIR],
                                             w[:, k * F:(k + 1) * F], start=(kk == 0 and p == 0),
                                             stop=(kk == KD - 1 and p == 1))
                else:
                    for k in range(2):
                        kk = 2 * (c % 2) + k
                        for half in range(2):
                            for p, w in enumerate(parts):
                                last = pe.matmul(ps[0:PAIR, 6 + half, :], h_split[:, kk * PAIR:(kk + 1) * PAIR],
                                                 w[:, k * D + half * 512:k * D + (half + 1) * 512],
                                                 start=(kk == 0 and p == 0), stop=(kk == 3 and p == 1))
                last.then_inc(w_used, 1)

            def fold_rows(e, n):
                pe.wait_ge(gu_ready, 2 * e + n + 1)
                for k in range(4):
                    last = pe.matmul(ps[:, 4, (4 * n + k) * TILE:(4 * n + k + 1) * TILE],
                                     gu_rows[:, n * F + k * P:n * F + (k + 1) * P], fold[0:PAIR], start=True, stop=True)
                last.then_inc(folded, 1)

            def stage(e, i, par, first=False, second=False, final=False):
                def next_product(c):
                    product(*parts_of(c, first), x_split[par], c, number(e, c, first))

                pe.wait_ge(x_lo_ready, e + 1)
                next_product(0)
                next_product(1)
                if not final:
                    pe.wait_ge(xg_in[1 - par], (i + par) * 16 + 16)
                    turn(xg[1 - par], 0)
                    turn(xg[1 - par], 1, xt_done)
                next_product(2)
                next_product(3)
                if not first:
                    pe.wait_ge(h_lo_ready, e)
                    if not second:
                        pe.wait_ge(y_ready, e - 1)
                    next_product(4)
                    next_product(5)
                for n in range(2):
                    fold_rows(e, n)

            pe.wait_ge(emptied["dve"], emptied_by("dve", NUM["rank"]))
            pe.wait_ge(consts, 2 + PAIR // TILE)
            pe.wait_ge(xg_in[0], 16)
            turn(xg[0], 0)
            turn(xg[0], 1, xt_done)
            stage(0, 0, 0, first=True)
            stage(1, 0, 1, second=True)
            with pe.Fori(1, NE // 2 - 1) as i:
                for par in range(2):
                    stage(2 * i + par, i, par)
            stage(NE - 2, NE // 2 - 1, 0)
            stage(NE - 1, NE // 2 - 1, 1, final=True)
            pe.wait_ge(h_lo_ready, NE)
            pe.wait_ge(y_ready, NE - 1)
            for c in (4, 5):
                product(w_hi[c % 3], w_lo[c % 3], None, c, 6 * NE - 6 + c)
            pe.wait_ge(counts_ready, 1)

            def more(i, row, n):
                e = n + (NE - 1)
                pe.wait_ge(xg_in[0], (n + NE // 2) * 16)
                turn(xg[0], 0)
                turn(xg[0], 1, xt_done)
                pe.wait_ge(x_lo_ready, e + 1)
                for c in range(4):
                    product(w_hi[c % 3], w_lo[c % 3], x_split[0], c, 6 * e + c)
                for k in range(2):
                    fold_rows(e, k)
                pe.wait_ge(h_lo_ready, e + 1)
                for c in range(4, 6):
                    product(w_hi[c % 3], w_lo[c % 3], None, c, 6 * e + c)

            overflow(pe, more)


_INS = ["x_prompt", "x_sample", "state_ssm_re", "state_ssm_im", "cache_pool", "g_mix", "w_in", "ssm_a_re",
        "ssm_a_im", "ssm_log_dt", "ssm_b_re", "ssm_b_im", "ssm_c_re", "ssm_c_im", "ssm_d", "w_glu_a", "w_glu_b",
        "pool_w", "pool_scale", "w_out", "g_ffn", "w_router_group", "w_router_expert", "w_exp_gate", "w_exp_up",
        "w_exp_down", "g_final"]
_OUTS = [("y_prompt", (1, SEQ, D)), ("y_sample", (1, DEC, D)), ("re_p", (1, 1, G, N)), ("im_p", (1, 1, G, N)),
         ("hist_p", (1, 1, HIST, 512)), ("re_s", (1, 1, G, N)), ("im_s", (1, 1, G, N)), ("hist_s", (1, 1, HIST, 512))]


def kernel(**inputs):
    import numpy as _np
    import concourse.bacc as _bacc
    from concourse import mybir as _mybir
    from concourse.bass_utils import run_bass_kernel_spmd as _run

    nc = _bacc.Bacc("TRN2", target_bir_lowering=False, num_devices=1)
    arrays, args, outs = {}, {}, {}
    for name in _INS:
        arr = _np.ascontiguousarray(inputs[name])
        arrays[f"in_{name}"] = arr
        args[name] = nc.dram_tensor(f"in_{name}", arr.shape, _mybir.dt.from_np(arr.dtype), kind="ExternalInput").ap()
    for name, shape in _OUTS:
        outs[name] = nc.dram_tensor(f"out_{name}", shape, F32, kind="ExternalOutput").ap()
    encoder_step(nc, args, outs)
    r = _run(nc, [arrays], core_ids=[0])
    return tuple(r.results[0][f"out_{name}"] for name, _ in _OUTS)
```
